# Optimizing a Trainium2 kernel written in Bass

```python
import math
import jax, jax.numpy as jnp
from jax import lax
import numpy as np

D_MODEL = 1024
BATCH = 1
SEQ = 512
DEPTH = 1

RET_HEADS = 4
RET_DK = 128
RET_DV = 128
RET_WIDTH = RET_HEADS * RET_DV
RET_CHUNK = 128
ROPE_BASE = 10000.0
DIFF_HEADS = 4
DIFF_DK = 64
DIFF_DV = 128
DIFF_WIDTH = DIFF_HEADS * DIFF_DV
Q_BLOCK = 128
MIX_WIDTH = RET_WIDTH + DIFF_WIDTH
COL_SIZES = (RET_HEADS * RET_DK, RET_HEADS * RET_DK, RET_WIDTH, RET_WIDTH,
             DIFF_HEADS * 2 * DIFF_DK, DIFF_HEADS * 2 * DIFF_DK, DIFF_WIDTH)
IN_COLS = sum(COL_SIZES)
COL_SPLITS = tuple(int(s) for s in np.cumsum(COL_SIZES)[:-1])
PEER_HEADS = 8
PEER_N_KEYS = 128
PEER_N_EXPERTS = PEER_N_KEYS * PEER_N_KEYS
PEER_D_QUERY = 256
PEER_D_HALF = PEER_D_QUERY // 2
PEER_TOPK = 16
PEER_TOKEN_CHUNK = 128
DEEPNORM_ALPHA = (2.0 * DEPTH) ** 0.25
DEEPNORM_BETA = (8.0 * DEPTH) ** -0.25
LN_EPS = 1e-5

kernel_name = "hymba_retnet_diffattn_peer_deepnorm"

def lambda_init(layer_idx):
    return 0.8 - 0.6 * math.exp(-0.3 * (layer_idx - 1))

def layer_norm(x, g, b):
    xf = x.astype(jnp.float32)
    mu = jnp.mean(xf, -1, keepdims=True)
    var = jnp.mean(jnp.square(xf - mu), -1, keepdims=True)
    return ((xf - mu) * lax.rsqrt(var + LN_EPS) * g + b).astype(x.dtype)

def rotary(x, pos):
    half = x.shape[-1] // 2
    inv = ROPE_BASE ** (-jnp.arange(half, dtype=jnp.float32) / half)
    ang = pos.astype(jnp.float32)[:, None] * inv[None, :]
    cos = jnp.cos(ang).astype(x.dtype)
    sin = jnp.sin(ang).astype(x.dtype)
    x1, x2 = x[..., :half], x[..., half:]
    return jnp.concatenate([x1 * cos - x2 * sin, x1 * sin + x2 * cos], axis=-1)

def retention_chunkwise(q, k, v):
    B, H, S, dk = q.shape
    dv = v.shape[-1]
    C = RET_CHUNK
    n = S // C
    qf, kf, vf = q.astype(jnp.float32), k.astype(jnp.float32) * dk ** -0.5, v.astype(jnp.float32)
    log_g = jnp.log1p(-(2.0 ** (-5.0 - jnp.arange(H, dtype=jnp.float32))))
    idx = jnp.arange(C, dtype=jnp.float32)
    rel = idx[:, None] - idx[None, :]
    decay_in = jnp.where(rel[None] >= 0, jnp.exp(jnp.maximum(rel, 0.0)[None] * log_g[:, None, None]), 0.0)
    decay_q = jnp.exp((idx + 1.0)[None, :] * log_g[:, None])
    decay_k = jnp.exp((C - 1.0 - idx)[None, :] * log_g[:, None])
    decay_c = jnp.exp(C * log_g)

    def to_chunks(t):
        return t.reshape(B, H, n, C, t.shape[-1]).transpose(2, 0, 1, 3, 4)

    def step(state, inp):
        qi, ki, vi = inp
        s = jnp.einsum('bhid,bhjd->bhij', qi, ki) * decay_in[None]
        inner = jnp.einsum('bhij,bhjv->bhiv', s, vi)
        cross = jnp.einsum('bhid,bhdv->bhiv', qi, state) * decay_q[None, :, :, None]
        state = state * decay_c[None, :, None, None] + jnp.einsum(
            'bhjd,bhjv->bhdv', ki * decay_k[None, :, :, None], vi)
        return state, inner + cross

    state0 = jnp.zeros((B, H, dk, dv), jnp.float32)
    _, out = lax.scan(step, state0, (to_chunks(qf), to_chunks(kf), to_chunks(vf)))
    return out.transpose(1, 2, 0, 3, 4).reshape(B, H, S, dv).astype(q.dtype)

def diff_attention(q, k, v, lam):
    B, H, _, S, dk = q.shape
    dv = v.shape[-1]
    nb = S // Q_BLOCK
    scale = dk ** -0.5
    kpos = jnp.arange(S)
    qb = q.reshape(B, H, 2, nb, Q_BLOCK, dk).transpose(3, 0, 1, 2, 4, 5)

    def block(args):
        qi, i = args
        s = jnp.einsum('bhcqd,bhckd->bhcqk', qi, k).astype(jnp.float32) * scale
        qpos = i * Q_BLOCK + jnp.arange(Q_BLOCK)
        mask = kpos[None, :] <= qpos[:, None]
        p = jax.nn.softmax(jnp.where(mask, s, -jnp.inf), axis=-1)
        a = p[:, :, 0] - lam * p[:, :, 1]
        return jnp.einsum('bhqk,bhkv->bhqv', a.astype(v.dtype), v)

    out = lax.map(block, (qb, jnp.arange(nb)))
    return out.transpose(1, 2, 0, 3, 4).reshape(B, H, S, dv)

def head_norm(o, g, b, rms_only):
    B, H, S, d = o.shape
    of = o.astype(jnp.float32)
    if rms_only:
        on = of * lax.rsqrt(jnp.mean(jnp.square(of), -1, keepdims=True) + LN_EPS)
    else:
        mu = jnp.mean(of, -1, keepdims=True)
        var = jnp.mean(jnp.square(of - mu), -1, keepdims=True)
        on = (of - mu) * lax.rsqrt(var + LN_EPS)
    on = on.transpose(0, 2, 1, 3).reshape(B, S, H * d) * g
    if b is not None:
        on = on + b
    return on.astype(o.dtype)

def hybrid_mixer(x, w_in, ret_gn_g, ret_gn_b, lq1, lk1, lq2, lk2, subln_g, w_out, lam_init):
    B, S, _ = x.shape
    pos = jnp.arange(S)
    proj = x @ w_in
    rq, rk, rv, rg, dq, dk, dv = jnp.split(proj, COL_SPLITS, axis=-1)
    heads = lambda t, d: t.reshape(B, S, -1, d).transpose(0, 2, 1, 3)
    r_out = retention_chunkwise(rotary(heads(rq, RET_DK), pos), rotary(heads(rk, RET_DK), pos),
                                heads(rv, RET_DV))
    r = jax.nn.silu(rg) * head_norm(r_out, ret_gn_g, ret_gn_b, rms_only=False)
    dq = dq.reshape(B, S, DIFF_HEADS, 2, DIFF_DK).transpose(0, 2, 3, 1, 4)
    dk = dk.reshape(B, S, DIFF_HEADS, 2, DIFF_DK).transpose(0, 2, 3, 1, 4)
    f32 = jnp.float32
    lam = (jnp.exp(jnp.sum(lq1.astype(f32) * lk1.astype(f32)))
           - jnp.exp(jnp.sum(lq2.astype(f32) * lk2.astype(f32))) + lam_init)
    d_out = diff_attention(dq, dk, heads(dv, DIFF_DV), lam)
    d = head_norm(d_out, subln_g, None, rms_only=True) * (1.0 - lam_init)
    return jnp.concatenate([r, d], axis=-1) @ w_out

def peer(x, w_query, sub_keys, expert_u, expert_v):
    B, S, D = x.shape
    T = B * S
    xt = x.reshape(T, D)
    q = (xt @ w_query).reshape(T, PEER_HEADS, 2, PEER_D_HALF)
    s = jnp.einsum('thcd,hckd->thck', q, sub_keys).astype(jnp.float32)
    top_s, top_i = lax.top_k(s, PEER_TOPK)
    cand_s = (top_s[:, :, 0, :, None] + top_s[:, :, 1, None, :]).reshape(T, PEER_HEADS, PEER_TOPK ** 2)
    cand_i = (top_i[:, :, 0, :, None] * PEER_N_KEYS + top_i[:, :, 1, None, :]).reshape(T, PEER_HEADS, PEER_TOPK ** 2)
    best_s, pos = lax.top_k(cand_s, PEER_TOPK)
    expert_idx = jnp.take_along_axis(cand_i, pos, axis=-1)
    gate = jax.nn.softmax(best_s, axis=-1)
    C = PEER_TOKEN_CHUNK
    nc = T // C
    E = PEER_HEADS * PEER_TOPK

    def chunk(args):
        xc, ic, gc = args
        u = jnp.take(expert_u, ic, axis=0)
        h = jax.nn.gelu(jnp.einsum('cd,ced->ce', xc, u).astype(jnp.float32), approximate=False)
        vv = jnp.take(expert_v, ic, axis=0)
        return jnp.einsum('ce,ced->cd', (gc * h).astype(vv.dtype), vv)

    out = lax.map(chunk, (xt.reshape(nc, C, D), expert_idx.reshape(nc, C, E), gate.reshape(nc, C, E)))
    return out.reshape(B, S, D).astype(x.dtype)

def setup_inputs(seed: int = 0) -> dict:
    key = jax.random.key(seed)
    ks = jax.random.split(key, 24)
    nrm = lambda k, shape, s: jax.random.normal(k, shape, jnp.float32) * s
    L = DEPTH
    beta = DEEPNORM_BETA
    col_scale = jnp.concatenate([
        jnp.full((COL_SIZES[0] + COL_SIZES[1],), 1.0),
        jnp.full((COL_SIZES[2],), beta),
        jnp.full((COL_SIZES[3] + COL_SIZES[4] + COL_SIZES[5],), 1.0),
        jnp.full((COL_SIZES[6],), beta),
    ]).astype(jnp.float32)
    w_in = nrm(ks[1], (L, D_MODEL, IN_COLS), D_MODEL ** -0.5) * col_scale
    return {
        "x": nrm(ks[0], (BATCH, SEQ, D_MODEL), 1.0),
        "w_in": w_in,
        "ret_gn_g": 1.0 + nrm(ks[2], (L, RET_WIDTH), 0.02),
        "ret_gn_b": nrm(ks[3], (L, RET_WIDTH), 0.02),
        "diff_lambda_q1": nrm(ks[4], (L, DIFF_DK), 0.1),
        "diff_lambda_k1": nrm(ks[5], (L, DIFF_DK), 0.1),
        "diff_lambda_q2": nrm(ks[6], (L, DIFF_DK), 0.1),
        "diff_lambda_k2": nrm(ks[7], (L, DIFF_DK), 0.1),
        "diff_subln_g": 1.0 + nrm(ks[8], (L, DIFF_WIDTH), 0.02),
        "w_out": nrm(ks[9], (L, MIX_WIDTH, D_MODEL), MIX_WIDTH ** -0.5 * beta),
        "ln1_g": 1.0 + nrm(ks[10], (L, D_MODEL), 0.02),
        "ln1_b": nrm(ks[11], (L, D_MODEL), 0.02),
        "peer_w_query": nrm(ks[12], (L, D_MODEL, PEER_HEADS * PEER_D_QUERY), D_MODEL ** -0.5),
        "peer_sub_keys": nrm(ks[13], (L, PEER_HEADS, 2, PEER_N_KEYS, PEER_D_HALF), PEER_D_HALF ** -0.5),
        "peer_u": nrm(ks[14], (L, PEER_N_EXPERTS, D_MODEL), D_MODEL ** -0.5),
        "peer_v": nrm(ks[15], (L, PEER_N_EXPERTS, D_MODEL), beta),
        "ln2_g": 1.0 + nrm(ks[16], (L, D_MODEL), 0.02),
        "ln2_b": nrm(ks[17], (L, D_MODEL), 0.02),
    }

def reference(x, w_in, ret_gn_g, ret_gn_b, diff_lambda_q1, diff_lambda_k1, diff_lambda_q2,
              diff_lambda_k2, diff_subln_g, w_out, ln1_g, ln1_b, peer_w_query, peer_sub_keys,
              peer_u, peer_v, ln2_g, ln2_b):
    for l in range(DEPTH):
        mix = hybrid_mixer(x, w_in[l], ret_gn_g[l], ret_gn_b[l], diff_lambda_q1[l], diff_lambda_k1[l],
                           diff_lambda_q2[l], diff_lambda_k2[l], diff_subln_g[l], w_out[l],
                           lambda_init(l + 1))
        x = layer_norm(DEEPNORM_ALPHA * x + mix, ln1_g[l], ln1_b[l])
        ffn = peer(x, peer_w_query[l], peer_sub_keys[l], peer_u[l], peer_v[l])
        x = layer_norm(DEEPNORM_ALPHA * x + ffn, ln2_g[l], ln2_b[l])
    return x


_drawn_inputs = setup_inputs


def setup_inputs(seed=0):
    import zlib

    import numpy as np

    out = dict(_drawn_inputs(seed))
    spreads = {}
    factors = {'ret_gn_g': 3.17, 'ret_gn_b': 3.066, 'diff_subln_g': 2.763, 'ln2_g': 2.856, 'ln2_b': 2.874}
    for name, (base, spread) in spreads.items():
        noise = np.random.default_rng([zlib.crc32(name.encode()), seed]).standard_normal(out[name].shape)
        drawn = base * np.exp(spread * noise) if base else spread * noise
        out[name] = __import__('jax').numpy.asarray(drawn.astype(out[name].dtype))
    for name, factor in factors.items():
        out[name] = (out[name] * factor).astype(out[name].dtype)
    return out
```

```python
import concourse.bass as bass
from concourse import mybir
from contextlib import ExitStack

fp32 = mybir.dt.float32
i32 = mybir.dt.int32
u32 = mybir.dt.uint32
ALU = mybir.AluOpType
ACT = mybir.ActivationFunctionType
AX = mybir.AxisListType

P = 128
S = 512
D = 1024
KD = D // P
NB = S // P
H = 4
HW = 512
DK = 64
HC = 16
PH = 8
TOPK = 16
E = PH * TOPK
ALPHA = 2.0 ** 0.25
LAMBDA_INIT = 0.8 - 0.6
EPS = 1e-5
LOWEST = -3.0e38
MASKED = -1.0e30
WAVES = [[0], [1, 2, 3]]
NW = 2
RING = 8
GROUPS = E // RING
RQ, RK, RV, RG, DQ, DKK, DV = range(7)
WIN, WOUT, WQ = 7, 2, 4
PER_WAVE = WIN + WOUT + WQ


def proj_fills():
    out = []
    for w, blocks in enumerate(WAVES):
        for g in range(WIN):
            if g in (DQ, DKK):
                out += [(w, g, h, "act") for h in (range(H) if w else [None])]
            else:
                out += [(w, g, b, "dve" if g in (RQ, RK, RG) else "act") for b in blocks]
    return out


FILLS = proj_fills()


def takes(n, who):
    return sum(f[3] == who for f in FILLS[:n])


def rots(n):
    return sum(f[1] in (RQ, RK) for f in FILLS[:n])


def gates(n):
    return sum(f[1] == RG for f in FILLS[:n])


def tiles_before(b):
    return b * (b + 1) // 2


def build(nc, x, xT, w_in, ret_gn_g, ret_gn_b, lq1, lk1, lq2, lk2, subln_g, w_out, ln1_g, ln1_b,
          w_query, keysT, peer_u, peer_v, ln2_g, ln2_b, decay, rope, ident_in, mask_in, decay_far, out):
    ctx = ExitStack()
    with ctx:
        def sb(name, shape, dt=fp32):
            return ctx.enter_context(nc.sbuf_tensor(name, shape, dt))

        def sem(name):
            return ctx.enter_context(nc.semaphore(name))

        wt = sb("wt", [P, NW, KD, HW])
        actT = sb("actT", [P, KD, S])
        xs = sb("xs", [P, NB, D])
        qT = sb("qT", [P, H, 3 * P])
        kT = sb("kT", [P, H, S])
        rv = sb("rv", [P, NB, HW])
        swish = sb("swish", [P, 3, HW])
        dqT = sb("dqT", [P, H, 3 * P])
        dkT = sb("dkT", [P, H, S])
        dv = sb("dv", [P, NB, HW])
        keys = sb("keys", [P, HC, P])
        dec = sb("dec", [P, 2, HW])
        rp = sb("rp", [P, 2, NB, 64])
        lng = sb("lng", [P, 2, D])
        gn = sb("gn", [P, 3, HW])
        ident = sb("ident", [P, P])
        mask = sb("mask", [P, P])
        ring = sb("ring", [P, RING, D])
        attn = sb("attn", [P, 3 * HW])
        probs = attn[:, 0:2 * HW].rearrange("p (c n) -> p c n", c=2)
        aT = attn[:, 2 * HW:3 * HW]
        qq = attn[:, :].rearrange("p (i t) -> p i t", i=4)
        wide = sb("wide", [P, 4 * HW])
        sT = wide[:, :].rearrange("p (j n) -> p j n", j=NB)
        mixT = wide[:, 0:D].rearrange("p (k t) -> p k t", k=KD)
        work = sb("work", [P, 2 * HW])
        best_v = sb("best_v", [P, 3, HC, TOPK])
        best_i = sb("best_i", [P, 3, HC, TOPK], u32)
        spare = sb("spare", [P, P])
        top_v = sb("top_v", [P, PH, TOPK])
        top_p = sb("top_p", [P, PH, TOPK], u32)
        half_f = sb("half_f", [P, HC, TOPK])
        pos_f = sb("pos_f", [P, E])
        sel = sb("sel", [P, 2, E])
        iota_i = sb("iota_i", [P, TOPK], i32)
        iota_f = sb("iota_f", [P, TOPK])
        idx = sb("idx", [P, 2, E], i32)
        gate = sb("gate", [P, 2, E])
        stage = sb("stage", [P, 2, RING], i32)
        hid = sb("hid", [P, E])
        wgt = sb("wgt", [P, E])
        st = sb("st", [P, 4, 6])
        mv = sb("mv", [P, 4, 2])
        rstd = sb("rstd", [P, 4])
        root = sb("root", [P, 2, 4])
        smax = sb("smax", [P, 2])
        nmax = sb("nmax", [P, 2])
        zsum = sb("zsum", [P, 2])
        rz = sb("rz", [P, 2])
        ssq = sb("ssq", [P, 4])
        lam_in = sb("lam_in", [P, 4, DK])
        lam = sb("lam", [P, 4])
        gsum = sb("gsum", [P, PH])

        W = ctx.enter_context(nc.psum_tensor("W", [P, 4, HW], fp32))
        X = ctx.enter_context(nc.psum_tensor("X", [P, D], fp32))
        ACC = ctx.enter_context(nc.psum_tensor("ACC", [P, D], fp32))

        w_landed = [sem(f"w_landed{i}") for i in range(NW)]
        xT_landed = sem("xT_landed")
        x_landed = sem("x_landed")
        rope_landed = sem("rope_landed")
        tabs_landed = sem("tabs_landed")
        lam_landed = sem("lam_landed")
        ln1_landed = sem("ln1_landed")
        ln2_landed = sem("ln2_landed")
        keys_landed = sem("keys_landed")
        row_landed = [sem(f"row_landed{i}") for i in range(RING)]
        stored = sem("stored")
        proj_ready = sem("proj_ready")
        rot_turned = sem("rot_turned")
        ret_scored = sem("ret_scored")
        ret_mixed = sem("ret_mixed")
        diff_scored = sem("diff_scored")
        a_turned = sem("a_turned")
        diff_mixed = sem("diff_mixed")
        mix_turned = sem("mix_turned")
        mixer_ready = sem("mixer_ready")
        x1_turned = sem("x1_turned")
        query_ready = sem("query_ready")
        keys_scored = sem("keys_scored")
        proj_taken_act = sem("proj_taken_act")
        tanh_ready = sem("tanh_ready")
        rot_taken = sem("rot_taken")
        exps_ready = sem("exps_ready")
        a_taken = sem("a_taken")
        squares_ready = sem("squares_ready")
        mix_taken = sem("mix_taken")
        x1_taken = sem("x1_taken")
        query_taken = sem("query_taken")
        token_in_psum = sem("token_in_psum")
        sum_started = sem("sum_started")
        gelu_ready = sem("gelu_ready")
        gate_exp_ready = sem("gate_exp_ready")
        lam_exp_ready = sem("lam_exp_ready")
        proj_taken_dve = sem("proj_taken_dve")
        rot_ready = sem("rot_ready")
        ret_decayed = sem("ret_decayed")
        ret_normed = sem("ret_normed")
        max_ready = sem("max_ready")
        a_ready = sem("a_ready")
        mix_ready = sem("mix_ready")
        x1_ready = sem("x1_ready")
        scores_taken = sem("scores_taken")
        gate_in_ready = sem("gate_in_ready")
        experts_ready = sem("experts_ready")
        row_used = sem("row_used")
        weights_ready = sem("weights_ready")
        block_done = sem("block_done")
        lam_dots_ready = sem("lam_dots_ready")
        dve_step = sem("dve_step")
        iota_ready = sem("iota_ready")
        staged = sem("staged")
        staged_tick = sem("slot_checked")

        block = ctx.enter_context(nc.Block())

        def wslot(w, i):
            n = w * PER_WAVE + i
            return n % NW, 16 * (n // NW + 1)

        @block.sync
        def _(sp):
            def wait_used(w, i):
                if i < WIN:
                    sp.wait_ge(proj_ready, sum(f[:2] <= (w, i) for f in FILLS))
                elif i < WIN + WOUT:
                    sp.wait_ge(mixer_ready, 2 * WAVES[w][-1] + i - WIN + 1)
                else:
                    s = i - WIN - WOUT
                    sp.wait_ge(query_ready, (4 + 4 * (s + 1)) if w else s + 1)

            def load_w(w, i):
                n = w * PER_WAVE + i
                if n >= NW:
                    wait_used(*divmod(n - NW, PER_WAVE))
                if i < WIN:
                    src = w_in[:, i * HW:(i + 1) * HW]
                elif i < WIN + WOUT:
                    src = w_out[:, (i - WIN) * HW:(i - WIN + 1) * HW]
                else:
                    j = i - WIN - WOUT
                    src = w_query[:, j * HW:(j + 1) * HW]
                src = src.rearrange("(k p) n -> p k n", p=P)
                sp.dma_start(wt[:, n % NW, :, :], src).then_inc(w_landed[n % NW], 16)

            sp.dma_start(actT[:], xT.rearrange("(k p) t -> p k t", p=P)).then_inc(xT_landed, 16)
            load_w(0, 0)
            sp.dma_start(rp[:], rope.rearrange("c (b p) n -> p c b n", p=P)).then_inc(rope_landed, 16)
            sp.dma_start(ident[:], ident_in).then_inc(rope_landed, 16)
            load_w(0, 1)
            for i, v in enumerate((lq1, lk1, lq2, lk2)):
                sp.dma_start(lam_in[:, i, :], v.partition_broadcast(P)).then_inc(lam_landed, 16)
            sp.dma_start(mask[:], mask_in).then_inc(tabs_landed, 16)
            sp.dma_start(dec[:], decay).then_inc(tabs_landed, 16)
            for i, v in enumerate((ret_gn_g, ret_gn_b, subln_g)):
                sp.dma_start(gn[:, i, :], v.partition_broadcast(P)).then_inc(tabs_landed, 16)
            load_w(0, 2)
            sp.dma_start(xs[:], x.rearrange("(b p) d -> p b d", p=P)).then_inc(x_landed, 16)
            load_w(0, 3)
            for i, v in enumerate((ln1_g, ln1_b)):
                sp.dma_start(lng[:, i, :], v.partition_broadcast(P)).then_inc(ln1_landed, 16)
            load_w(0, 4)
            sp.dma_start(keys[:], keysT).then_inc(keys_landed, 16)
            for i in range(5, PER_WAVE):
                load_w(0, i)
            for i in range(PER_WAVE):
                load_w(1, i)
            sp.wait_ge(x1_ready, NB)
            for i, v in enumerate((ln2_g, ln2_b)):
                sp.dma_start(lng[:, i, :], v.partition_broadcast(P)).then_inc(ln2_landed, 16)
            for b in range(NB):
                sp.wait_ge(block_done, b + 1)
                sp.dma_start(out[b * P:(b + 1) * P, :], xs[:, b, :]).then_inc(stored, 16)
            sp.wait_ge(stored, 16 * NB)

        @block.gpsimd
        def _(pool):
            nc.gpsimd.iota(iota_i[:], pattern=[[1, TOPK]], base=0, channel_multiplier=0).then_inc(iota_ready, 1)
            for b in range(NB):
                pool.wait_ge(experts_ready, b + 1)
                for ph, table in enumerate((peer_u, peer_v)):
                    at = (2 * b + ph) * E
                    with pool.Fori(0, GROUPS // 2) as i:
                        for odd in range(2):
                            pool.wait_ge(row_used, i * 2 * RING + odd * RING + at + 1)
                            nc.gpsimd.tensor_copy(
                                stage[:, odd, :], idx[:, b % 2, bass.ds(i * 2 * RING + odd * RING, RING)]
                            ).then_inc(staged, 1)
                            pool.wait_ge(staged, i * 2 + odd + 1 + (2 * b + ph) * GROUPS)
                            for r in range(RING):
                                pool.wait_ge(row_used, i * 2 * RING + odd * RING + r + at + 1)
                                nc.gpsimd.sem_inc(staged_tick, 1)
                                pool.indirect_dma_start(
                                    out=ring[:, r, :], out_offset=None, in_=table,
                                    in_offset=bass.IndirectOffsetOnAxis(ap=stage[:, odd, r:r + 1], axis=0),
                                ).then_inc(row_landed[r], 16)

        @block.tensor
        def _(pe):
            fill = [0]

            def turn(n):
                pe.wait_ge(rot_ready, n + 1)
                if n:
                    pe.wait_ge(rot_taken, n)
                for h in range(H):
                    last = nc.tensor.transpose(W[:, 3, h * P:(h + 1) * P], work[:, h * P:(h + 1) * P], ident[:])
                last.then_inc(rot_turned, 1)

            def project(w, blocks):
                toks = slice(blocks[0] * P, (blocks[-1] + 1) * P)
                n_tok = len(blocks) * P
                turned = 0
                for g in range(WIN):
                    slot, landed = wslot(w, g)
                    pe.wait_ge(w_landed[slot], landed)
                    wide_tile = g in (DQ, DKK)
                    parts = (range(H) if w else [None]) if wide_tile else blocks
                    for part in parts:
                        n = fill[0]
                        assert FILLS[n][:3] == (w, g, part)
                        if n >= 3:
                            who = FILLS[n - 3][3]
                            pe.wait_ge(proj_taken_act if who == "act" else proj_taken_dve, takes(n - 2, who))
                        bank = W[:, n % 3, :]
                        if not wide_tile:
                            for k in range(KD):
                                last = nc.tensor.matmul(bank, actT[:, k, part * P:(part + 1) * P],
                                                        wt[:, slot, k, :], start=(k == 0), stop=(k == KD - 1))
                        else:
                            for h in (range(H) if part is None else [part]):
                                at = h * P if part is None else 0
                                for k in range(KD):
                                    last = nc.tensor.matmul(bank[:, at:at + n_tok], wt[:, slot, k, h * P:(h + 1) * P],
                                                            actT[:, k, toks], start=(k == 0), stop=(k == KD - 1))
                        last.then_inc(proj_ready, 1)
                        fill[0] += 1
                        if n and FILLS[n - 1][0] == w and FILLS[n - 1][1] in (RQ, RK):
                            turn(rots(n) - 1)
                return

            def retention(w, b):
                q = b - WAVES[w][0]
                for jb in range(b + 1):
                    n = tiles_before(b) + jb
                    if jb < 2:
                        if b in (0, 1):
                            pe.wait_ge(proj_taken_act, takes(fill[0], "act"))
                            pe.wait_ge(proj_taken_dve, takes(fill[0], "dve"))
                            pe.wait_ge(rot_taken, rots(fill[0]))
                        else:
                            pe.wait_ge(x1_taken, 2 * b)
                    else:
                        pe.wait_ge(ret_decayed, n - 1)
                    for h in range(H):
                        last = nc.tensor.matmul(W[:, jb % 2, h * P:(h + 1) * P], kT[:, h, jb * P:(jb + 1) * P],
                                                qT[:, h, q * P:(q + 1) * P], start=True, stop=True)
                    last.then_inc(ret_scored, 1)
                pe.wait_ge(ret_decayed, tiles_before(b + 1))
                if b > 1:
                    pe.wait_ge(x1_ready, b)
                for h in range(H):
                    for jb in range(b + 1):
                        last = nc.tensor.matmul(W[:, 2, h * P:(h + 1) * P], sT[:, jb, h * P:(h + 1) * P],
                                                rv[:, jb, h * P:(h + 1) * P], start=(jb == 0), stop=(jb == b))
                last.then_inc(ret_mixed, 1)

            def diff(w, b):
                q = b - WAVES[w][0]
                keys_n = (b + 1) * P

                def score(h):
                    if h:
                        pe.wait_ge(exps_ready, H * b + h)
                    for c in range(2):
                        last = nc.tensor.matmul(W[:, c, 0:keys_n], dqT[c * DK:(c + 1) * DK, h, q * P:(q + 1) * P],
                                                dkT[c * DK:(c + 1) * DK, h, 0:keys_n], start=True, stop=True)
                    last.then_inc(diff_scored, 1)

                score(0)
                for h in range(H):
                    if h < H - 1:
                        score(h + 1)
                    n = H * b + h
                    pe.wait_ge(a_ready, n + 1)
                    if n and h:
                        pe.wait_ge(a_taken, n)
                    for kb in range(b + 1):
                        last = nc.tensor.transpose(W[:, 3, kb * P:(kb + 1) * P], probs[:, 0, kb * P:(kb + 1) * P], ident[:])
                    last.then_inc(a_turned, 1)
                    pe.wait_ge(a_taken, n + 1)
                    if h == 0:
                        pe.wait_ge(ret_normed, b + 1)
                    for kb in range(b + 1):
                        last = nc.tensor.matmul(W[:, 2, h * P:(h + 1) * P], aT[:, kb * P:(kb + 1) * P],
                                                dv[:, kb, h * P:(h + 1) * P], start=(kb == 0), stop=(kb == b))
                last.then_inc(diff_mixed, 1)

            def mixer_out(w, b):
                pe.wait_ge(mix_ready, b + 1)
                for half in range(2):
                    for k in range(4):
                        c = 4 * half + k
                        last = nc.tensor.transpose(W[:, half, k * P:(k + 1) * P], work[:, c * P:(c + 1) * P], ident[:])
                    last.then_inc(mix_turned, 1)
                pe.wait_ge(mix_taken, 2 * (b + 1))
                for half in range(2):
                    slot, landed = wslot(w, WIN + half)
                    pe.wait_ge(w_landed[slot], landed)
                    for k in range(KD):
                        last = nc.tensor.matmul(W[:, 2 + half, :], mixT[:, k, :], wt[:, slot, k, :],
                                                start=(k == 0), stop=(k == KD - 1))
                    last.then_inc(mixer_ready, 1)
                pe.wait_ge(x1_ready, b + 1)
                for half in range(2):
                    for k in range(4):
                        c = 4 * half + k
                        last = nc.tensor.transpose(W[:, half, k * P:(k + 1) * P], xs[:, b, c * P:(c + 1) * P], ident[:])
                    last.then_inc(x1_turned, 1)

            def query(w, blocks):
                n_tok = len(blocks) * P
                toks = slice(blocks[0] * P, (blocks[-1] + 1) * P)
                pe.wait_ge(x1_taken, 2 * (blocks[-1] + 1))
                pe.wait_ge(keys_landed, 16)
                fq = 16 if w else 4
                for s in range(WQ):
                    slot, landed = wslot(w, WIN + WOUT + s)
                    pe.wait_ge(w_landed[slot], landed)
                    for i in range(4):
                        n = (4 + 4 * s + i) if w else s
                        if (w or i == 0) and n - (4 if w else 0) >= 2:
                            pe.wait_ge(query_taken, n - 1)
                        dst = W[:, 2 + n % 2, 0:n_tok] if w else W[:, 2 + n % 2, i * P:(i + 1) * P]
                        for k in range(KD):
                            last = nc.tensor.matmul(dst, wt[:, slot, k, i * P:(i + 1) * P], actT[:, k, toks],
                                                    start=(k == 0), stop=(k == KD - 1))
                        if w or i == 3:
                            last.then_inc(query_ready, 1)
                    pe.wait_ge(query_taken, (4 + 4 * (s + 1)) if w else s + 1)
                    for j in range(len(blocks)):
                        n = (4 if w else 0) + s * len(blocks) + j
                        if n - (4 if w else 0) >= 2:
                            pe.wait_ge(scores_taken, n - 1)
                        for i in range(4):
                            last = nc.tensor.matmul(W[:, n % 2, i * P:(i + 1) * P], qq[:, i, j * P:(j + 1) * P],
                                                    keys[:, 4 * s + i, :], start=True, stop=True)
                        last.then_inc(keys_scored, 1)

            pe.wait_ge(xT_landed, 16)
            pe.wait_ge(rope_landed, 32)
            for w, blocks in enumerate(WAVES):
                if w:
                    pe.wait_ge(scores_taken, 4)
                    pe.wait_ge(experts_ready, 1)
                project(w, blocks)
                for b in blocks:
                    retention(w, b)
                    diff(w, b)
                    mixer_out(w, b)
                query(w, blocks)

        @block.scalar
        def _(act):
            fill = [0]

            def take_rotated(w):
                n = rotated[0]
                f = [f for f in FILLS if f[1] in (RQ, RK)][n]
                act.wait_ge(rot_turned, n + 1)
                b = f[2]
                q = b - WAVES[w][0]
                dst = qT[:, :, q * P:(q + 1) * P] if f[1] == RQ else kT[:, :, b * P:(b + 1) * P]
                nc.scalar.activation(dst, W[:, 3, :].rearrange("p (h t) -> p h t", h=H), ACT.Copy).then_inc(rot_taken, 1)
                rotated[0] += 1

            rotated = [0]

            def project(w, blocks):
                n_tok = len(blocks) * P
                toks = slice(blocks[0] * P, (blocks[-1] + 1) * P)
                for f in [f for f in FILLS if f[0] == w]:
                    n = fill[0]
                    g, part = f[1], f[2]
                    bank = W[:, n % 3, :]
                    if g == RG:
                        act.wait_ge(proj_ready, n + 1)
                        act.wait_ge(rot_ready, rots(n))
                        act.wait_ge(proj_taken_dve, takes(n, "dve"))
                        nc.scalar.activation(work[:, HW:2 * HW], bank, ACT.Tanh, scale=0.5).then_inc(tanh_ready, 1)
                    elif g not in (RQ, RK):
                        act.wait_ge(proj_ready, n + 1)
                        if g == RV:
                            dst, src = rv[:, part, :], bank
                        elif g == DV:
                            dst, src = dv[:, part, :], bank
                        elif part is None:
                            src = bank.rearrange("p (h t) -> p h t", h=H)
                            dst = dqT[:, :, 0:P] if g == DQ else dkT[:, :, 0:P]
                        else:
                            src = bank[:, 0:n_tok]
                            dst = dqT[:, part, :] if g == DQ else dkT[:, part, toks]
                        nc.scalar.activation(dst, src, ACT.Copy).then_inc(proj_taken_act, 1)
                    fill[0] += 1
                    if n and FILLS[n - 1][0] == w and FILLS[n - 1][1] in (RQ, RK):
                        take_rotated(w)

            def attention(w, b):
                keys_n = (b + 1) * P
                for h in range(H):
                    n = H * b + h
                    act.wait_ge(max_ready, n + 1)
                    if h:
                        act.wait_ge(a_turned, n)
                    for c in range(2):
                        last = nc.scalar.activation(probs[:, c, 0:keys_n], W[:, c, 0:keys_n], ACT.Exp,
                                                    bias=nmax[:, c:c + 1], scale=DK ** -0.5, accum_out=zsum[:, c:c + 1])
                    last.then_inc(exps_ready, 1)
                    act.wait_ge(a_turned, n + 1)
                    nc.scalar.activation(aT[:, 0:keys_n], W[:, 3, 0:keys_n], ACT.Copy).then_inc(a_taken, 1)
                act.wait_ge(diff_mixed, b + 1)
                for h in range(H):
                    last = nc.scalar.activation(probs[:, 1, h * P:(h + 1) * P], W[:, 2, h * P:(h + 1) * P], ACT.Square,
                                                accum_out=ssq[:, h:h + 1])
                last.then_inc(squares_ready, 1)
                for half in range(2):
                    act.wait_ge(mix_turned, 2 * b + half + 1)
                    nc.scalar.activation(mixT[:, 4 * half:4 * half + 4, :],
                                         W[:, half, :].rearrange("p (k t) -> p k t", k=4), ACT.Copy).then_inc(mix_taken, 1)
                for half in range(2):
                    act.wait_ge(x1_turned, 2 * b + half + 1)
                    nc.scalar.activation(actT[:, 4 * half:4 * half + 4, b * P:(b + 1) * P],
                                         W[:, half, :].rearrange("p (k t) -> p k t", k=4), ACT.Copy).then_inc(x1_taken, 1)

            def query(w, blocks):
                n_tok = len(blocks) * P
                for n in range(4, 20) if w else range(4):
                    act.wait_ge(query_ready, n + 1)
                    if w and n % 4 == 0 and n > 4:
                        act.wait_ge(keys_scored, 4 + (n // 4 - 1) * 3)
                    if not w and n:
                        act.wait_ge(keys_scored, n)
                    src = W[:, 2 + n % 2, :]
                    if w:
                        dst, src = qq[:, n % 4, 0:n_tok], src[:, 0:n_tok]
                    else:
                        dst, src = qq[:, :, 0:P], src.rearrange("p (i t) -> p i t", i=4)
                    nc.scalar.activation(dst, src, ACT.Copy).then_inc(query_taken, 1)

            def gate_exp(b):
                act.wait_ge(gate_in_ready, b + 1)
                nc.scalar.activation(gate[:, b % 2, :], pos_f[:], ACT.Exp).then_inc(gate_exp_ready, 1)

            def token_to_psum(b):
                act.wait_ge(x1_ready, b + 1)
                if b:
                    act.wait_ge(row_used, RING + (2 * b - 1) * E)
                for half in range(2):
                    last = nc.scalar.activation(X[:, half * HW:(half + 1) * HW], xs[:, b, half * HW:(half + 1) * HW],
                                                ACT.Copy)
                last.then_inc(token_in_psum, 1)

            def start_sum(b):
                if b:
                    act.wait_ge(block_done, b)
                for half in range(2):
                    last = nc.scalar.activation(ACC[:, half * HW:(half + 1) * HW], xs[:, b, half * HW:(half + 1) * HW],
                                                ACT.Copy, scale=ALPHA)
                last.then_inc(sum_started, 1)

            def gelu(b):
                act.wait_ge(row_used, RING + (2 * b + 1) * E)
                if b:
                    act.wait_ge(row_used, RING + 2 * b * E)
                nc.scalar.activation(wgt[:], hid[:], ACT.Gelu).then_inc(gelu_ready, 1)

            act.wait_ge(lam_dots_ready, 1)
            nc.scalar.activation(lam[:, 2:4], lam[:, 0:2], ACT.Exp).then_inc(lam_exp_ready, 1)
            project(0, WAVES[0])
            attention(0, 0)
            token_to_psum(0)
            start_sum(0)
            query(0, WAVES[0])
            gate_exp(0)
            project(1, WAVES[1])
            attention(1, 1)
            gelu(0)
            token_to_psum(1)
            attention(1, 2)
            attention(1, 3)
            query(1, WAVES[1])
            gate_exp(1)
            start_sum(1)
            for b in range(1, NB):
                if b + 1 < NB:
                    gate_exp(b + 1)
                gelu(b)
                if b + 1 < NB:
                    token_to_psum(b + 1)
                    start_sum(b + 1)

        @block.vector
        def _(dve):
            steps = [0]

            def link(ins):
                steps[0] += 1
                ins.then_inc(dve_step, 1)
                dve.wait_ge(dve_step, steps[0])

            TT = nc.vector.tensor_tensor
            TS = nc.vector.tensor_scalar
            STT = nc.vector.scalar_tensor_tensor

            def dots(b, lo, hi):
                def one(i, r):
                    dve.wait_ge(row_landed[r], i * 16 + 16 * (2 * b * GROUPS + 1))
                    STT(out=ring[:, r, :], in0=ring[:, r, :], scalar=1.0, in1=X[:], op0=ALU.mult, op1=ALU.mult,
                        accum_out=hid[:, bass.ds(i * RING + r, 1)]).then_inc(row_used, 1)
                if lo == 0:
                    dve.wait_ge(token_in_psum, b + 1)
                    if b:
                        dve.wait_ge(weights_ready, b)
                if hi - lo == 1:
                    for r in range(RING):
                        one(lo, r)
                else:
                    with dve.Fori(lo, hi) as i:
                        for r in range(RING):
                            one(i, r)

            def sums(b, lo, hi):
                def one(i, r):
                    dve.wait_ge(row_landed[r], i * 16 + 16 * ((2 * b + 1) * GROUPS + 1))
                    dve.wait_ge(row_used, i * RING + r + RING + (2 * b + 1) * E)
                    STT(out=ACC[:], in0=ring[:, r, :], scalar=wgt[:, bass.ds(i * RING + r, 1)], in1=ACC[:],
                        op0=ALU.mult, op1=ALU.add).then_inc(row_used, 1)
                if hi - lo == 1:
                    for r in range(RING):
                        one(lo, r)
                else:
                    with dve.Fori(lo, hi) as i:
                        for r in range(RING):
                            one(i, r)

            def weights(b):
                dve.wait_ge(gelu_ready, b + 1)
                TT(out=wgt[:], in0=wgt[:], in1=gate[:, b % 2, :], op=ALU.mult).then_inc(weights_ready, 1)
                dve.wait_ge(weights_ready, b + 1)
                dve.wait_ge(sum_started, b + 1)

            def inverse_root(n):
                v, y, t = rstd[:, 0:n], root[:, 0, 0:n], root[:, 1, 0:n]
                link(TS(t.bitcast(i32), v.bitcast(i32), 1, None, ALU.arith_shift_right))
                link(TS(y.bitcast(i32), t.bitcast(i32), -1.0, float(0x5F3759DF), ALU.mult, ALU.add))
                for step in range(3):
                    link(TT(out=t, in0=y, in1=y, op=ALU.mult))
                    link(TT(out=t, in0=t, in1=v, op=ALU.mult))
                    link(TS(t, t, -0.5, 1.5, ALU.mult, ALU.add))
                    link(TT(out=v if step == 2 else y, in0=y, in1=t, op=ALU.mult))

            def normalise(b, src, gain_bias):
                for half in range(2):
                    link(nc.vector.bn_stats(st[:, half, :], src[:, half * HW:(half + 1) * HW]))
                link(nc.vector.bn_aggr(mv[:, 0, :], st[:, 0:2, :].rearrange("p a b -> p (a b)")))
                link(TS(rstd[:, 0:1], mv[:, 0, 1:2], EPS, None, ALU.add))
                inverse_root(1)
                link(TS(xs[:, b, :], src, mv[:, 0, 0:1], rstd[:, 0:1], ALU.subtract, ALU.mult))
                link(TT(out=xs[:, b, :], in0=xs[:, b, :], in1=gain_bias[:, 0, :], op=ALU.mult))
                return TT(out=xs[:, b, :], in0=xs[:, b, :], in1=gain_bias[:, 1, :], op=ALU.add)

            def finish(b):
                dve.wait_ge(row_used, RING + (2 * b + 2) * E)
                dve.wait_ge(ln2_landed, 32)
                normalise(b, ACC[:], lng).then_inc(block_done, 1)

            proj = [f for f in enumerate(FILLS)]

            def rotary(n):
                b = FILLS[n][2]
                src = W[:, n % 3, :].rearrange("p (h n) -> p h n", h=H)
                a = work[:, 0:HW].rearrange("p (h n) -> p h n", h=H)
                t = work[:, HW:2 * HW].rearrange("p (h n) -> p h n", h=H)
                cos = rp[:, 0, b, :].unsqueeze(1).to_broadcast([P, H, 64])
                sin = rp[:, 1, b, :].unsqueeze(1).to_broadcast([P, H, 64])
                dve.wait_ge(proj_ready, n + 1)
                if rots(n):
                    dve.wait_ge(rot_turned, rots(n))
                link(TT(out=a[:, :, 0:64], in0=src[:, :, 0:64], in1=cos, op=ALU.mult))
                link(TT(out=a[:, :, 64:P], in0=src[:, :, 64:P], in1=cos, op=ALU.mult))
                link(TT(out=t[:, :, 0:64], in0=src[:, :, 64:P], in1=sin, op=ALU.mult))
                TT(out=t[:, :, 64:P], in0=src[:, :, 0:64], in1=sin, op=ALU.mult).then_inc(proj_taken_dve, 1)
                dve.wait_ge(proj_taken_dve, takes(n + 1, "dve"))
                link(TT(out=a[:, :, 0:64], in0=a[:, :, 0:64], in1=t[:, :, 0:64], op=ALU.subtract))
                TT(out=a[:, :, 64:P], in0=a[:, :, 64:P], in1=t[:, :, 64:P], op=ALU.add).then_inc(rot_ready, 1)

            def swish_gate(n):
                w, b = FILLS[n][0], FILLS[n][2]
                dve.wait_ge(tanh_ready, gates(n) + 1)
                STT(out=swish[:, b - WAVES[w][0], :], in0=work[:, HW:2 * HW], scalar=1.0, in1=W[:, n % 3, :],
                    op0=ALU.add, op1=ALU.mult).then_inc(proj_taken_dve, 1)

            def fills_of(w, g):
                return [n for n, f in enumerate(FILLS) if f[0] == w and f[1] == g]

            def decay_scores(b):
                for jb in range(b + 1):
                    off = b - jb
                    dve.wait_ge(ret_scored, tiles_before(b) + jb + 1)
                    if off < 2:
                        TT(out=sT[:, jb, :], in0=W[:, jb % 2, :], in1=dec[:, off, :], op=ALU.mult).then_inc(ret_decayed, 1)
                    else:
                        for h in range(H):
                            ins = STT(out=sT[:, jb, h * P:(h + 1) * P], in0=W[:, jb % 2, h * P:(h + 1) * P],
                                      scalar=decay_far[h] ** (off - 1), in1=dec[:, 1, h * P:(h + 1) * P],
                                      op0=ALU.mult, op1=ALU.mult)
                        ins.then_inc(ret_decayed, 1)

            def retention_norm(w, b):
                dve.wait_ge(ret_mixed, b + 1)
                for h in range(H):
                    link(nc.vector.bn_stats(st[:, h, :], W[:, 2, h * P:(h + 1) * P]))
                for h in range(H):
                    link(nc.vector.bn_aggr(mv[:, h, :], st[:, h, :]))
                link(TS(rstd[:], mv[:, :, 1], EPS, None, ALU.add))
                inverse_root(H)
                for h in range(H):
                    ins = TS(work[:, h * P:(h + 1) * P], W[:, 2, h * P:(h + 1) * P], mv[:, h, 0:1], rstd[:, h:h + 1],
                             ALU.subtract, ALU.mult)
                    if h == H - 1:
                        ins.then_inc(ret_normed, 1)
                dve.wait_ge(ret_normed, b + 1)
                link(TT(out=work[:, 0:HW], in0=work[:, 0:HW], in1=gn[:, 0, :], op=ALU.mult))
                link(TT(out=work[:, 0:HW], in0=work[:, 0:HW], in1=gn[:, 1, :], op=ALU.add))
                link(TT(out=work[:, 0:HW], in0=work[:, 0:HW], in1=swish[:, b - WAVES[w][0], :], op=ALU.mult))

            def softmax_max(b, h):
                keys_n = (b + 1) * P
                dve.wait_ge(diff_scored, H * b + h + 1)
                link(TT(out=W[:, 0:2, b * P:keys_n], in0=W[:, 0:2, b * P:keys_n],
                        in1=mask[:].unsqueeze(1).to_broadcast([P, 2, P]), op=ALU.add))
                link(nc.vector.reduce_max(smax[:], W[:, 0:2, 0:keys_n], AX.X))
                TS(nmax[:], smax[:], -DK ** -0.5, None, ALU.mult).then_inc(max_ready, 1)

            def softmax_join(b, h):
                keys_n = (b + 1) * P
                dve.wait_ge(exps_ready, H * b + h + 1)
                link(nc.vector.reciprocal(rz[:], zsum[:]))
                link(TS(rz[:, 1:2], rz[:, 1:2], lam[:, 0:1], None, ALU.mult))
                link(TS(probs[:, 1, 0:keys_n], probs[:, 1, 0:keys_n], rz[:, 1:2], None, ALU.mult))
                STT(out=probs[:, 0, 0:keys_n], in0=probs[:, 0, 0:keys_n], scalar=rz[:, 0:1], in1=probs[:, 1, 0:keys_n],
                    op0=ALU.mult, op1=ALU.add).then_inc(a_ready, 1)

            def diff_norm(b):
                dve.wait_ge(squares_ready, b + 1)
                link(TS(rstd[:], ssq[:], 1.0 / P, EPS, ALU.mult, ALU.add))
                inverse_root(H)
                for h in range(H):
                    ins = STT(out=work[:, HW + h * P:HW + (h + 1) * P], in0=W[:, 2, h * P:(h + 1) * P],
                              scalar=rstd[:, h:h + 1], in1=gn[:, 2, h * P:(h + 1) * P], op0=ALU.mult, op1=ALU.mult)
                ins.then_inc(mix_ready, 1)

            def ln1(b):
                dve.wait_ge(mixer_ready, 2 * (b + 1))
                link(STT(out=xs[:, b, :], in0=xs[:, b, :], scalar=ALPHA, in1=W[:, 2:4, :].rearrange("p a n -> p (a n)"),
                         op0=ALU.mult, op1=ALU.add))
                normalise(b, xs[:, b, :], lng).then_inc(x1_ready, 1)

            def best_keys(w, s, j):
                n = (4 if w else 0) + s * len(WAVES[w]) + j
                dve.wait_ge(keys_scored, n + 1)
                for i in range(4):
                    sc = W[:, n % 2, i * P:(i + 1) * P]
                    v, ix = best_v[:, j, 4 * s + i, :], best_i[:, j, 4 * s + i, :]
                    link(nc.vector.max(v[:, 0:8], sc))
                    link(nc.vector.max_index(ix[:, 0:8], v[:, 0:8], sc))
                    ins = nc.vector.match_replace(spare[:], v[:, 0:8], sc, LOWEST)
                    link(ins)
                    if i == 3:
                        nc.vector.sem_inc(scores_taken, 1)
                    link(nc.vector.max(v[:, 8:16], spare[:]))
                    link(nc.vector.max_index(ix[:, 8:16], v[:, 8:16], spare[:]))

            def best_experts(w, b):
                j = b - WAVES[w][0]
                v = best_v[:, j, :, :].rearrange("p (h c) k -> p h c k", c=2)
                cand = wide[:].rearrange("p (h a b) -> p h a b", h=PH, a=TOPK)
                link(TT(out=cand, in0=v[:, :, 0, :].unsqueeze(3).to_broadcast([P, PH, TOPK, TOPK]),
                        in1=v[:, :, 1, :].unsqueeze(2).to_broadcast([P, PH, TOPK, TOPK]), op=ALU.add))
                for h in range(PH):
                    c = wide[:, h * 256:(h + 1) * 256]
                    link(nc.vector.max(top_v[:, h, 0:8], c))
                    link(nc.vector.max_index(top_p[:, h, 0:8], top_v[:, h, 0:8], c))
                    link(nc.vector.match_replace(c, top_v[:, h, 0:8], c, LOWEST))
                    link(nc.vector.max(top_v[:, h, 8:16], c))
                    link(nc.vector.max_index(top_p[:, h, 8:16], top_v[:, h, 8:16], c))
                link(nc.vector.tensor_copy(half_f[:], best_i[:, j, :, :]))
                i_f = half_f[:].rearrange("p (h c) k -> p h c k", c=2)
                onehot = wide[:].rearrange("p (e a) -> p e a", a=TOPK)
                pick = wide[:].rearrange("p (h k a) -> p h k a", h=PH, k=TOPK)
                top_pf = top_p[:].rearrange("p h k -> p (h k)")
                if b == 0:
                    dve.wait_ge(iota_ready, 1)
                    link(nc.vector.tensor_copy(iota_f[:], iota_i[:]))
                for c, (op, arg) in enumerate(((ALU.logical_shift_right, 4), (ALU.bitwise_and, 15))):
                    link(TS(spare[:].bitcast(u32), top_pf, arg, None, op))
                    link(nc.vector.tensor_copy(pos_f[:], spare[:].bitcast(u32)))
                    link(TT(out=onehot, in0=pos_f[:].unsqueeze(2).to_broadcast([P, E, TOPK]),
                            in1=iota_f[:].unsqueeze(1).to_broadcast([P, E, TOPK]), op=ALU.is_equal))
                    link(TT(out=pick, in0=pick, in1=i_f[:, :, c, :].unsqueeze(2).to_broadcast([P, PH, TOPK, TOPK]),
                            op=ALU.mult))
                    link(nc.vector.reduce_sum(sel[:, c, :], onehot, AX.X))
                if b >= 2:
                    dve.wait_ge(staged, (2 * (b - 2) + 2) * GROUPS)
                STT(out=idx[:, b % 2, :], in0=sel[:, 0, :], scalar=float(P), in1=sel[:, 1, :],
                    op0=ALU.mult, op1=ALU.add).then_inc(experts_ready, 1)
                TT(out=pos_f[:].rearrange("p (h k) -> p h k", h=PH), in0=top_v[:],
                   in1=top_v[:, :, 0:1].to_broadcast([P, PH, TOPK]), op=ALU.subtract).then_inc(gate_in_ready, 1)
                dve.wait_ge(gate_exp_ready, b + 1)
                g = gate[:, b % 2, :].rearrange("p (h k) -> p h k", h=PH)
                link(nc.vector.reduce_sum(gsum[:], g, AX.X))
                link(nc.vector.reciprocal(gsum[:], gsum[:]))
                link(TT(out=g, in0=g, in1=gsum[:].unsqueeze(2).to_broadcast([P, PH, TOPK]), op=ALU.mult))

            nc.vector.sem_inc(row_used, RING)
            dve.wait_ge(lam_landed, 64)
            lam_v = lam_in[:].rearrange("p (a b) n -> p a b n", b=2)
            link(TT(out=lam_v[:, :, 0, :], in0=lam_v[:, :, 0, :], in1=lam_v[:, :, 1, :], op=ALU.mult))
            nc.vector.reduce_sum(lam[:, 0:2], lam_v[:, :, 0, :], AX.X).then_inc(lam_dots_ready, 1)
            dve.wait_ge(lam_exp_ready, 1)
            link(TT(out=lam[:, 1:2], in0=lam[:, 3:4], in1=lam[:, 2:3], op=ALU.subtract))
            link(TS(lam[:, 0:1], lam[:, 1:2], -LAMBDA_INIT, None, ALU.add))
            dve.wait_ge(tabs_landed, 5 * 16)
            link(TS(gn[:, 0:2, :], gn[:, 0:2, :], 0.5, None, ALU.mult))
            link(TS(gn[:, 2, :], gn[:, 2, :], 1.0 - LAMBDA_INIT, None, ALU.mult))
            dve.wait_ge(rope_landed, 32)

            rotary(fills_of(0, RQ)[0])
            rotary(fills_of(0, RK)[0])
            swish_gate(fills_of(0, RG)[0])

            decay_scores(0)
            retention_norm(0, 0)
            for h in range(H):
                softmax_max(0, h)
                softmax_join(0, h)
            diff_norm(0)
            dve.wait_ge(x_landed, 16)
            dve.wait_ge(ln1_landed, 32)
            ln1(0)
            for s in range(WQ):
                best_keys(0, s, 0)
            best_experts(0, 0)

            g = 0
            for n in fills_of(1, RQ) + fills_of(1, RK):
                rotary(n)
                dots(0, g, g + 1)
                g += 1
            for n in fills_of(1, RG):
                swish_gate(n)
                dots(0, g, g + 1)
                g += 1
            decay_scores(1)
            dots(0, g, g + 1)
            retention_norm(1, 1)
            dots(0, g + 1, g + 2)
            g += 2
            for h in range(H):
                softmax_max(1, h)
                softmax_join(1, h)
                if h < 3:
                    dots(0, g, g + 1)
                    g += 1
            dots(0, g, GROUPS)
            diff_norm(1)
            ln1(1)
            weights(0)
            g = 0
            for b in (2, 3):
                decay_scores(b)
                sums(0, g, g + 1)
                retention_norm(1, b)
                sums(0, g + 1, g + 2)
                g += 2
                for h in range(H):
                    softmax_max(b, h)
                    softmax_join(b, h)
                    if h % 2:
                        sums(0, g, g + 1)
                        g += 1
                diff_norm(b)
                sums(0, g, g + 1)
                ln1(b)
                g += 1
            for s in range(WQ):
                for j in range(3):
                    best_keys(1, s, j)
                    if (s * 3 + j) % 2 and g < GROUPS:
                        sums(0, g, g + 1)
                        g += 1
            assert g == GROUPS
            best_experts(1, 1)
            finish(0)

            for b in range(1, NB):
                dots(b, 0, 4)
                if b + 1 < NB:
                    best_experts(1, b + 1)
                dots(b, 4, GROUPS)
                weights(b)
                sums(b, 0, GROUPS)
                finish(b)


def constants():
    import numpy as np
    log_g = np.log1p(-(2.0 ** (-5.0 - np.arange(H))))
    i = np.arange(P)
    rel = (i[None, :] - i[:, None])[:, None, :]
    near = np.where(rel >= 0, np.exp(np.maximum(rel, 0) * log_g[None, :, None]), 0.0)
    far = np.exp((rel + P) * log_g[None, :, None])
    decay = (np.stack([near, far], axis=1) * P ** -0.5).reshape(P, 2, HW)
    ang = np.arange(S)[:, None] * (10000.0 ** (-np.arange(64) / 64.0))[None, :]
    rope = np.stack([np.cos(ang), np.sin(ang)])
    mask = np.where(i[None, :] > i[:, None], MASKED, 0.0)
    f = np.float32
    return {"decay": decay.astype(f), "rope": rope.astype(f), "ident_in": np.eye(P, dtype=f),
            "mask_in": mask.astype(f)}, [float(v) for v in np.exp(P * log_g)]


INPUTS = ["x", "xT", "w_in", "ret_gn_g", "ret_gn_b", "diff_lambda_q1", "diff_lambda_k1", "diff_lambda_q2",
          "diff_lambda_k2", "diff_subln_g", "w_out", "ln1_g", "ln1_b", "peer_w_query", "keysT", "peer_u",
          "peer_v", "ln2_g", "ln2_b", "decay", "rope", "ident_in", "mask_in"]


def kernel(**inputs):
    import numpy as np
    import concourse.bacc as bacc
    from concourse.bass_utils import run_bass_kernel_spmd

    given = {n: np.asarray(a)[0] for n, a in inputs.items()}
    given["xT"] = given["x"].T
    given["keysT"] = given["peer_sub_keys"].transpose(3, 0, 1, 2).reshape(P, HC, P)
    tables, decay_far = constants()
    given.update(tables)
    nc = bacc.Bacc("TRN2", target_bir_lowering=False, num_devices=1)
    arrays, aps = {}, []
    for name in INPUTS:
        a = np.ascontiguousarray(given[name])
        arrays[name] = a
        aps.append(nc.dram_tensor(name, a.shape, mybir.dt.from_np(a.dtype), kind="ExternalInput").ap())
    out = nc.dram_tensor("out", (S, D), fp32, kind="ExternalOutput").ap()
    build(nc, *aps, decay_far, out)
    r = run_bass_kernel_spmd(nc, [arrays], core_ids=[0])
    return r.results[0]["out"].reshape(1, S, D)
```

```python
import concourse.bass as bass
from concourse import mybir
from contextlib import ExitStack

fp32 = mybir.dt.float32
i32 = mybir.dt.int32
u32 = mybir.dt.uint32
ALU = mybir.AluOpType
ACT = mybir.ActivationFunctionType
AX = mybir.AxisListType

P = 128
S = 512
D = 1024
KD = D // P
NB = S // P
H = 4
HW = 512
DK = 64
HC = 16
PH = 8
TOPK = 16
E = PH * TOPK
ALPHA = 2.0 ** 0.25
LAMBDA_INIT = 0.8 - 0.6
EPS = 1e-5
LOWEST = -3.0e38
MASKED = -1.0e30
WAVES = [[0], [1, 2, 3]]
NW = 2
RING = 8
GROUPS = E // RING
QUARTER = GROUPS // 4
PE_ROWS = [[], [1, 3, 5, 7], [1, 3, 5, 7], [1, 3, 5, 7]]
RQ, RK, RV, RG, DQ, DKK, DV = range(7)
WIN, WOUT, WQ = 7, 2, 4
PER_WAVE = WIN + WOUT + WQ


def proj_fills():
    out = []
    for w, blocks in enumerate(WAVES):
        for g in range(WIN):
            if g in (DQ, DKK):
                out += [(w, g, h, "act") for h in (range(H) if w else [None])]
            else:
                out += [(w, g, b, "dve" if g in (RQ, RK, RG) else "act") for b in blocks]
    return out


FILLS = proj_fills()


def takes(n, who):
    return sum(f[3] == who for f in FILLS[:n])


def rots(n):
    return sum(f[1] in (RQ, RK) for f in FILLS[:n])


def gates(n):
    return sum(f[1] == RG for f in FILLS[:n])


def tiles_before(b):
    return b * (b + 1) // 2


def dve_rows(b):
    return [r for r in range(RING) if r not in PE_ROWS[b]]


def diags_before(b):
    return GROUPS * sum(len(PE_ROWS[i]) for i in range(b))


def build(nc, x, xT, w_in, ret_gn_g, ret_gn_b, lq1, lk1, lq2, lk2, subln_g, w_out, ln1_g, ln1_b,
          w_query, keysT, peer_u, peer_v, ln2_g, ln2_b, decay, rope, ident_in, mask_in, decay_far, out):
    ctx = ExitStack()
    with ctx:
        def sb(name, shape, dt=fp32):
            return ctx.enter_context(nc.sbuf_tensor(name, shape, dt))

        def sem(name):
            return ctx.enter_context(nc.semaphore(name))

        wt = sb("wt", [P, NW, KD, HW])
        actT = sb("actT", [P, KD, S])
        xs = sb("xs", [P, NB, D])
        qT = sb("qT", [P, H, 3 * P])
        kT = sb("kT", [P, H, S])
        rv = sb("rv", [P, NB, HW])
        swish = sb("swish", [P, 3, HW])
        dqT = sb("dqT", [P, H, 3 * P])
        dkT = sb("dkT", [P, H, S])
        dv = sb("dv", [P, NB, HW])
        keys = sb("keys", [P, HC, P])
        dec = sb("dec", [P, 2, HW])
        rp = sb("rp", [P, 2, NB, 64])
        lng = sb("lng", [P, 2, D])
        gn = sb("gn", [P, 3, HW])
        ident = sb("ident", [P, P])
        mask = sb("mask", [P, P])
        ring = sb("ring", [P, RING, D])
        attn = sb("attn", [P, 3 * HW])
        probs = attn[:, 0:2 * HW].rearrange("p (c n) -> p c n", c=2)
        aT = attn[:, 2 * HW:3 * HW]
        qq = attn[:, :].rearrange("p (i t) -> p i t", i=4)
        wide = sb("wide", [P, 4 * HW])
        sT = wide[:, :].rearrange("p (j n) -> p j n", j=NB)
        mixT = wide[:, 0:D].rearrange("p (k t) -> p k t", k=KD)
        work = sb("work", [P, 2 * HW])
        best_v = sb("best_v", [P, 4, TOPK])
        best_i = sb("best_i", [P, 4, TOPK], u32)
        cand = sb("cand", [P, 2 * TOPK * TOPK])
        top_v = sb("top_v", [P, 2, TOPK])
        top_p = sb("top_p", [P, 2 * TOPK], u32)
        half_f = sb("half_f", [P, 4, TOPK])
        pos_u = sb("pos_u", [P, 2, 2 * TOPK], u32)
        pos_f = sb("pos_f", [P, 2, 2 * TOPK])
        sel = sb("sel", [P, 2, 2 * TOPK])
        iota_i = sb("iota_i", [P, TOPK], i32)
        iota_f = sb("iota_f", [P, TOPK])
        idx = sb("idx", [P, NB, E], i32)
        gate = sb("gate", [P, NB, E])
        gexp = sb("gexp", [P, E])
        diag = sb("diag", [P, max(map(len, PE_ROWS)), P])
        stage = sb("stage", [P, 2, RING], i32)
        hid = sb("hid", [P, E])
        wgt = sb("wgt", [P, E])
        st = sb("st", [P, 4, 6])
        mv = sb("mv", [P, 4, 2])
        rstd = sb("rstd", [P, 4])
        root = sb("root", [P, 2, 4])
        smax = sb("smax", [P, 2])
        nmax = sb("nmax", [P, 2])
        zsum = sb("zsum", [P, 2])
        rz = sb("rz", [P, 2])
        ssq = sb("ssq", [P, 4])
        lam_in = sb("lam_in", [P, 4, DK])
        lam = sb("lam", [P, 4])
        gsum = sb("gsum", [P, PH])

        scores = {0: wide[:], 1: rv[:].rearrange("p b n -> p (b n)"), 2: kT[:].rearrange("p h n -> p (h n)"),
                  3: dkT[:].rearrange("p h n -> p (h n)")}

        W = ctx.enter_context(nc.psum_tensor("W", [P, 4, HW], fp32))
        X = ctx.enter_context(nc.psum_tensor("X", [P, D], fp32))
        ACC = ctx.enter_context(nc.psum_tensor("ACC", [P, D], fp32))

        w_landed = [sem(f"w_landed{i}") for i in range(NW)]
        xT_landed = sem("xT_landed")
        xT_rest_landed = sem("xT_rest_landed")
        x_landed = sem("x_landed")
        x_rest_landed = sem("x_rest_landed")
        rope_landed = sem("rope_landed")
        tabs_landed = sem("tabs_landed")
        lam_landed = sem("lam_landed")
        ln1_landed = sem("ln1_landed")
        ln2_landed = sem("ln2_landed")
        keys_landed = sem("keys_landed")
        row_landed = [sem(f"row_landed{i}") for i in range(RING)]
        stored = sem("stored")
        proj_ready = sem("proj_ready")
        rot_turned = sem("rot_turned")
        ret_scored = sem("ret_scored")
        ret_mixed = sem("ret_mixed")
        diff_scored = sem("diff_scored")
        a_turned = sem("a_turned")
        diff_mixed = sem("diff_mixed")
        mix_turned = sem("mix_turned")
        mixer_ready = sem("mixer_ready")
        x1_turned = sem("x1_turned")
        query_ready = sem("query_ready")
        keys_scored = sem("keys_scored")
        proj_taken_act = sem("proj_taken_act")
        tanh_ready = sem("tanh_ready")
        rot_taken = sem("rot_taken")
        exps_ready = sem("exps_ready")
        a_taken = sem("a_taken")
        squares_ready = sem("squares_ready")
        mix_taken = sem("mix_taken")
        x1_taken = sem("x1_taken")
        query_taken = sem("query_taken")
        token_in_psum = sem("token_in_psum")
        gelu_ready = sem("gelu_ready")
        gate_exp_ready = sem("gate_exp_ready")
        scores_stored = sem("scores_stored")
        diag_ready = sem("diag_ready")
        lam_exp_ready = sem("lam_exp_ready")
        diag_tick = sem("diag_slot_checked")
        proj_taken_dve = sem("proj_taken_dve")
        rot_ready = sem("rot_ready")
        ret_decayed = sem("ret_decayed")
        ret_normed = sem("ret_normed")
        max_ready = sem("max_ready")
        a_ready = sem("a_ready")
        mix_ready = sem("mix_ready")
        x1_ready = sem("x1_ready")
        experts_ready = sem("experts_ready")
        slot_used = [sem(f"slot_used{i}") for i in range(RING)]
        weights_ready = sem("weights_ready")
        low_added = sem("low_added")
        sum_read = sem("sum_read")
        block_done = sem("block_done")
        lam_dots_ready = sem("lam_dots_ready")
        dve_step = sem("dve_step")
        iota_ready = sem("iota_ready")
        staged = sem("staged")
        staged_tick = sem("slot_checked")

        block = ctx.enter_context(nc.Block())

        def wslot(w, i):
            n = w * PER_WAVE + i
            return n % NW, 16 * (n // NW + 1)

        @block.sync
        def _(sp):
            def wait_used(w, i):
                if i < WIN:
                    sp.wait_ge(proj_ready, sum(f[:2] <= (w, i) for f in FILLS))
                elif i < WIN + WOUT:
                    sp.wait_ge(mixer_ready, 2 * WAVES[w][-1] + i - WIN + 1)
                else:
                    s = i - WIN - WOUT
                    sp.wait_ge(query_ready, (4 + 4 * (s + 1)) if w else s + 1)

            def load_w(w, i):
                n = w * PER_WAVE + i
                if n >= NW:
                    wait_used(*divmod(n - NW, PER_WAVE))
                if i < WIN:
                    src = w_in[:, i * HW:(i + 1) * HW]
                elif i < WIN + WOUT:
                    src = w_out[:, (i - WIN) * HW:(i - WIN + 1) * HW]
                else:
                    j = i - WIN - WOUT
                    src = w_query[:, j * HW:(j + 1) * HW]
                src = src.rearrange("(k p) n -> p k n", p=P)
                sp.dma_start(wt[:, n % NW, :, :], src).then_inc(w_landed[n % NW], 16)

            xT_k = xT.rearrange("(k p) t -> p k t", p=P)
            x_b = x.rearrange("(b p) d -> p b d", p=P)
            sp.dma_start(actT[:, :, 0:P], xT_k[:, :, 0:P]).then_inc(xT_landed, 16)
            load_w(0, 0)
            sp.dma_start(rp[:], rope.rearrange("c (b p) n -> p c b n", p=P)).then_inc(rope_landed, 16)
            sp.dma_start(ident[:], ident_in).then_inc(rope_landed, 16)
            for i in range(1, WIN):
                load_w(0, i)
            for i, v in enumerate((lq1, lk1, lq2, lk2)):
                sp.dma_start(lam_in[:, i, :], v.partition_broadcast(P)).then_inc(lam_landed, 16)
            sp.dma_start(mask[:], mask_in).then_inc(tabs_landed, 16)
            sp.dma_start(dec[:], decay).then_inc(tabs_landed, 16)
            for i, v in enumerate((ret_gn_g, ret_gn_b, subln_g)):
                sp.dma_start(gn[:, i, :], v.partition_broadcast(P)).then_inc(tabs_landed, 16)
            load_w(0, WIN)
            sp.dma_start(xs[:, 0, :], x_b[:, 0, :]).then_inc(x_landed, 16)
            load_w(0, WIN + 1)
            for i, v in enumerate((ln1_g, ln1_b)):
                sp.dma_start(lng[:, i, :], v.partition_broadcast(P)).then_inc(ln1_landed, 16)
            sp.dma_start(keys[:], keysT).then_inc(keys_landed, 16)
            load_w(0, WIN + WOUT)
            sp.dma_start(actT[:, :, P:S], xT_k[:, :, P:S]).then_inc(xT_rest_landed, 16)
            load_w(0, WIN + WOUT + 1)
            sp.dma_start(xs[:, 1:NB, :], x_b[:, 1:NB, :]).then_inc(x_rest_landed, 16)
            for i in range(WIN + WOUT + 2, PER_WAVE):
                load_w(0, i)
            for i in range(PER_WAVE):
                load_w(1, i)
            sp.wait_ge(x1_ready, NB)
            for i, v in enumerate((ln2_g, ln2_b)):
                sp.dma_start(lng[:, i, :], v.partition_broadcast(P)).then_inc(ln2_landed, 16)
            for b in range(NB):
                sp.wait_ge(block_done, b + 1)
                sp.dma_start(out[b * P:(b + 1) * P, :], xs[:, b, :]).then_inc(stored, 16)
            sp.wait_ge(stored, 16 * NB)

        @block.gpsimd
        def _(pool):
            nc.gpsimd.iota(iota_i[:], pattern=[[1, TOPK]], base=0, channel_multiplier=0).then_inc(iota_ready, 1)
            for r in range(RING):
                nc.gpsimd.sem_inc(slot_used[r], 1)
            for b in range(NB):
                for ph, table in enumerate((peer_u, peer_v)):
                    before = (2 * b + ph) * GROUPS
                    with pool.Fori(0, 4) as quarter:
                        pool.wait_ge(experts_ready, quarter + 4 * b + 1)
                        for j in range(QUARTER):
                            nc.gpsimd.tensor_copy(
                                stage[:, j % 2, :], idx[:, b, bass.ds(quarter * QUARTER * RING + j * RING, RING)]
                            ).then_inc(staged, 1)
                            pool.wait_ge(staged, quarter * QUARTER + j + 1 + before)
                            for r in range(RING):
                                pool.wait_ge(slot_used[r], quarter * QUARTER + j + 1 + before)
                                nc.gpsimd.sem_inc(staged_tick, 1)
                                pool.indirect_dma_start(
                                    out=ring[:, r, :], out_offset=None, in_=table,
                                    in_offset=bass.IndirectOffsetOnAxis(ap=stage[:, j % 2, r:r + 1], axis=0),
                                ).then_inc(row_landed[r], 16)

        @block.tensor
        def _(pe):
            fill = [0]

            def turn(n):
                pe.wait_ge(rot_ready, n + 1)
                if n:
                    pe.wait_ge(rot_taken, n)
                for h in range(H):
                    last = nc.tensor.transpose(W[:, 3, h * P:(h + 1) * P], work[:, h * P:(h + 1) * P], ident[:])
                last.then_inc(rot_turned, 1)

            def project(w, blocks):
                toks = slice(blocks[0] * P, (blocks[-1] + 1) * P)
                n_tok = len(blocks) * P
                turned = 0
                for g in range(WIN):
                    slot, landed = wslot(w, g)
                    pe.wait_ge(w_landed[slot], landed)
                    wide_tile = g in (DQ, DKK)
                    parts = (range(H) if w else [None]) if wide_tile else blocks
                    for part in parts:
                        n = fill[0]
                        assert FILLS[n][:3] == (w, g, part)
                        if n >= 3:
                            who = FILLS[n - 3][3]
                            pe.wait_ge(proj_taken_act if who == "act" else proj_taken_dve, takes(n - 2, who))
                        bank = W[:, n % 3, :]
                        if not wide_tile:
                            for k in range(KD):
                                last = nc.tensor.matmul(bank, actT[:, k, part * P:(part + 1) * P],
                                                        wt[:, slot, k, :], start=(k == 0), stop=(k == KD - 1))
                        else:
                            for h in (range(H) if part is None else [part]):
                                at = h * P if part is None else 0
                                for k in range(KD):
                                    last = nc.tensor.matmul(bank[:, at:at + n_tok], wt[:, slot, k, h * P:(h + 1) * P],
                                                            actT[:, k, toks], start=(k == 0), stop=(k == KD - 1))
                        last.then_inc(proj_ready, 1)
                        fill[0] += 1
                        if n and FILLS[n - 1][0] == w and FILLS[n - 1][1] in (RQ, RK):
                            turn(rots(n) - 1)
                return

            def retention(w, b):
                q = b - WAVES[w][0]
                for jb in range(b + 1):
                    n = tiles_before(b) + jb
                    if jb < 2:
                        if b in (0, 1):
                            pe.wait_ge(proj_taken_act, takes(fill[0], "act"))
                            pe.wait_ge(proj_taken_dve, takes(fill[0], "dve"))
                            pe.wait_ge(rot_taken, rots(fill[0]))
                        else:
                            pe.wait_ge(x1_taken, 2 * b)
                    else:
                        pe.wait_ge(ret_decayed, n - 1)
                    for h in range(H):
                        last = nc.tensor.matmul(W[:, jb % 2, h * P:(h + 1) * P], kT[:, h, jb * P:(jb + 1) * P],
                                                qT[:, h, q * P:(q + 1) * P], start=True, stop=True)
                    last.then_inc(ret_scored, 1)
                pe.wait_ge(ret_decayed, tiles_before(b + 1))
                if b > 1:
                    pe.wait_ge(x1_ready, b)
                for h in range(H):
                    for jb in range(b + 1):
                        last = nc.tensor.matmul(W[:, 2, h * P:(h + 1) * P], sT[:, jb, h * P:(h + 1) * P],
                                                rv[:, jb, h * P:(h + 1) * P], start=(jb == 0), stop=(jb == b))
                last.then_inc(ret_mixed, 1)

            def diff(w, b):
                q = b - WAVES[w][0]
                keys_n = (b + 1) * P

                def score(h):
                    if h:
                        pe.wait_ge(exps_ready, H * b + h)
                    for c in range(2):
                        last = nc.tensor.matmul(W[:, c, 0:keys_n], dqT[c * DK:(c + 1) * DK, h, q * P:(q + 1) * P],
                                                dkT[c * DK:(c + 1) * DK, h, 0:keys_n], start=True, stop=True)
                    last.then_inc(diff_scored, 1)

                score(0)
                for h in range(H):
                    if h < H - 1:
                        score(h + 1)
                    n = H * b + h
                    pe.wait_ge(a_ready, n + 1)
                    if n and h:
                        pe.wait_ge(a_taken, n)
                    for kb in range(b + 1):
                        last = nc.tensor.transpose(W[:, 3, kb * P:(kb + 1) * P], probs[:, 0, kb * P:(kb + 1) * P], ident[:])
                    last.then_inc(a_turned, 1)
                    pe.wait_ge(a_taken, n + 1)
                    if h == 0:
                        pe.wait_ge(ret_normed, b + 1)
                    for kb in range(b + 1):
                        last = nc.tensor.matmul(W[:, 2, h * P:(h + 1) * P], aT[:, kb * P:(kb + 1) * P],
                                                dv[:, kb, h * P:(h + 1) * P], start=(kb == 0), stop=(kb == b))
                last.then_inc(diff_mixed, 1)

            def mixer_out(w, b):
                pe.wait_ge(mix_ready, b + 1)
                for half in range(2):
                    for k in range(4):
                        c = 4 * half + k
                        last = nc.tensor.transpose(W[:, half, k * P:(k + 1) * P], work[:, c * P:(c + 1) * P], ident[:])
                    last.then_inc(mix_turned, 1)
                pe.wait_ge(mix_taken, 2 * (b + 1))
                for half in range(2):
                    slot, landed = wslot(w, WIN + half)
                    pe.wait_ge(w_landed[slot], landed)
                    for k in range(KD):
                        last = nc.tensor.matmul(W[:, 2 + half, :], mixT[:, k, :], wt[:, slot, k, :],
                                                start=(k == 0), stop=(k == KD - 1))
                    last.then_inc(mixer_ready, 1)
                pe.wait_ge(x1_ready, b + 1)
                for half in range(2):
                    for k in range(4):
                        c = 4 * half + k
                        last = nc.tensor.transpose(W[:, half, k * P:(k + 1) * P], xs[:, b, c * P:(c + 1) * P], ident[:])
                    last.then_inc(x1_turned, 1)

            def query(w, blocks):
                n_tok = len(blocks) * P
                toks = slice(blocks[0] * P, (blocks[-1] + 1) * P)
                pe.wait_ge(x1_taken, 2 * (blocks[-1] + 1))
                pe.wait_ge(keys_landed, 16)
                fq = 16 if w else 4
                for s in range(WQ):
                    slot, landed = wslot(w, WIN + WOUT + s)
                    pe.wait_ge(w_landed[slot], landed)
                    for i in range(4):
                        n = (4 + 4 * s + i) if w else s
                        if (w or i == 0) and n - (4 if w else 0) >= 2:
                            pe.wait_ge(query_taken, n - 1)
                        dst = W[:, 2 + n % 2, 0:n_tok] if w else W[:, 2 + n % 2, i * P:(i + 1) * P]
                        for k in range(KD):
                            last = nc.tensor.matmul(dst, wt[:, slot, k, i * P:(i + 1) * P], actT[:, k, toks],
                                                    start=(k == 0), stop=(k == KD - 1))
                        if w or i == 3:
                            last.then_inc(query_ready, 1)
                    pe.wait_ge(query_taken, (4 + 4 * (s + 1)) if w else s + 1)
                    for j in range(len(blocks)):
                        n = (4 if w else 0) + s * len(blocks) + j
                        if n - (4 if w else 0) >= 2:
                            pe.wait_ge(scores_stored, n - 1)
                        for i in range(4):
                            last = nc.tensor.matmul(W[:, n % 2, i * P:(i + 1) * P], qq[:, i, j * P:(j + 1) * P],
                                                    keys[:, 4 * s + i, :], start=True, stop=True)
                        last.then_inc(keys_scored, 1)

            def add_rows(b):
                rows = PE_ROWS[b]

                def group(i, start, stop):
                    for m, r in enumerate(rows):
                        pe.wait_ge(row_landed[r], i * 16 + 16 * ((2 * b + 1) * GROUPS + 1))
                        pe.wait_ge(diag_ready, i * len(rows) + m + 1 + diags_before(b))
                        for half in range(2):
                            last = nc.tensor.matmul(
                                ACC[:, half * HW:(half + 1) * HW], diag[:, m, :], ring[:, r, half * HW:(half + 1) * HW],
                                start=start and m == 0, stop=stop and m == len(rows) - 1)
                        last.then_inc(slot_used[r], 1)

                if b and PE_ROWS[b - 1]:
                    pe.wait_ge(sum_read, sum(bool(PE_ROWS[i]) for i in range(b)))
                group(0, True, False)
                with pe.Fori(1, GROUPS - 1) as i:
                    group(i, False, False)
                group(GROUPS - 1, False, True)

            pe.wait_ge(xT_landed, 16)
            pe.wait_ge(rope_landed, 32)
            for w, blocks in enumerate(WAVES):
                if w:
                    pe.wait_ge(scores_stored, 4)
                    pe.wait_ge(xT_rest_landed, 16)
                project(w, blocks)
                for b in blocks:
                    retention(w, b)
                    diff(w, b)
                    mixer_out(w, b)
                query(w, blocks)
            for b in range(1, NB):
                add_rows(b)

        @block.scalar
        def _(act):
            fill = [0]

            def take_rotated(w):
                n = rotated[0]
                f = [f for f in FILLS if f[1] in (RQ, RK)][n]
                act.wait_ge(rot_turned, n + 1)
                b = f[2]
                q = b - WAVES[w][0]
                dst = qT[:, :, q * P:(q + 1) * P] if f[1] == RQ else kT[:, :, b * P:(b + 1) * P]
                nc.scalar.activation(dst, W[:, 3, :].rearrange("p (h t) -> p h t", h=H), ACT.Copy).then_inc(rot_taken, 1)
                rotated[0] += 1

            rotated = [0]

            def project(w, blocks):
                n_tok = len(blocks) * P
                toks = slice(blocks[0] * P, (blocks[-1] + 1) * P)
                for f in [f for f in FILLS if f[0] == w]:
                    n = fill[0]
                    g, part = f[1], f[2]
                    bank = W[:, n % 3, :]
                    if g == RG:
                        act.wait_ge(proj_ready, n + 1)
                        act.wait_ge(rot_ready, rots(n))
                        act.wait_ge(proj_taken_dve, takes(n, "dve"))
                        nc.scalar.activation(work[:, HW:2 * HW], bank, ACT.Tanh, scale=0.5).then_inc(tanh_ready, 1)
                    elif g not in (RQ, RK):
                        act.wait_ge(proj_ready, n + 1)
                        if g == RV:
                            dst, src = rv[:, part, :], bank
                        elif g == DV:
                            dst, src = dv[:, part, :], bank
                        elif part is None:
                            src = bank.rearrange("p (h t) -> p h t", h=H)
                            dst = dqT[:, :, 0:P] if g == DQ else dkT[:, :, 0:P]
                        else:
                            src = bank[:, 0:n_tok]
                            dst = dqT[:, part, :] if g == DQ else dkT[:, part, toks]
                        nc.scalar.activation(dst, src, ACT.Copy).then_inc(proj_taken_act, 1)
                    fill[0] += 1
                    if n and FILLS[n - 1][0] == w and FILLS[n - 1][1] in (RQ, RK):
                        take_rotated(w)

            def attention(w, b):
                keys_n = (b + 1) * P
                for h in range(H):
                    n = H * b + h
                    act.wait_ge(max_ready, n + 1)
                    if h:
                        act.wait_ge(a_turned, n)
                    for c in range(2):
                        last = nc.scalar.activation(probs[:, c, 0:keys_n], W[:, c, 0:keys_n], ACT.Exp,
                                                    bias=nmax[:, c:c + 1], scale=DK ** -0.5, accum_out=zsum[:, c:c + 1])
                    last.then_inc(exps_ready, 1)
                    act.wait_ge(a_turned, n + 1)
                    nc.scalar.activation(aT[:, 0:keys_n], W[:, 3, 0:keys_n], ACT.Copy).then_inc(a_taken, 1)
                act.wait_ge(diff_mixed, b + 1)
                for h in range(H):
                    last = nc.scalar.activation(probs[:, 1, h * P:(h + 1) * P], W[:, 2, h * P:(h + 1) * P], ACT.Square,
                                                accum_out=ssq[:, h:h + 1])
                last.then_inc(squares_ready, 1)
                for half in range(2):
                    act.wait_ge(mix_turned, 2 * b + half + 1)
                    nc.scalar.activation(mixT[:, 4 * half:4 * half + 4, :],
                                         W[:, half, :].rearrange("p (k t) -> p k t", k=4), ACT.Copy).then_inc(mix_taken, 1)
                for half in range(2):
                    act.wait_ge(x1_turned, 2 * b + half + 1)
                    nc.scalar.activation(actT[:, 4 * half:4 * half + 4, b * P:(b + 1) * P],
                                         W[:, half, :].rearrange("p (k t) -> p k t", k=4), ACT.Copy).then_inc(x1_taken, 1)

            def query(w, blocks):
                n_tok = len(blocks) * P
                for n in range(4, 20) if w else range(4):
                    act.wait_ge(query_ready, n + 1)
                    if w and n % 4 == 0 and n > 4:
                        act.wait_ge(keys_scored, 4 + (n // 4 - 1) * 3)
                    if not w and n:
                        act.wait_ge(keys_scored, n)
                    src = W[:, 2 + n % 2, :]
                    if w:
                        dst, src = qq[:, n % 4, 0:n_tok], src[:, 0:n_tok]
                    else:
                        dst, src = qq[:, :, 0:P], src.rearrange("p (i t) -> p i t", i=4)
                    nc.scalar.activation(dst, src, ACT.Copy).then_inc(query_taken, 1)
                    if not w or n % 4 == 3:
                        s = n // 4 - 1 if w else n
                        for j, b in enumerate(blocks):
                            m = (4 + 3 * s if w else s) + j
                            act.wait_ge(keys_scored, m + 1)
                            nc.scalar.activation(scores[b][:, s * HW:(s + 1) * HW], W[:, m % 2, :],
                                                 ACT.Copy).then_inc(scores_stored, 1)

            def token_to_psum(b):
                act.wait_ge(x1_ready, b + 1)
                if b:
                    act.wait_ge(slot_used[RING - 1], (2 * b - 1) * GROUPS + 1)
                for half in range(2):
                    last = nc.scalar.activation(X[:, half * HW:(half + 1) * HW], xs[:, b, half * HW:(half + 1) * HW],
                                                ACT.Copy)
                last.then_inc(token_in_psum, 1)

            def gelu(b):
                act.wait_ge(experts_ready, 4 * b + 4)
                if b:
                    act.wait_ge(weights_ready, b)
                nc.scalar.activation(gexp[:], gate[:, b, :], ACT.Exp).then_inc(gate_exp_ready, 1)
                act.wait_ge(slot_used[RING - 1], (2 * b + 1) * GROUPS + 1)
                if b:
                    act.wait_ge(slot_used[dve_rows(b - 1)[-1]], 2 * b * GROUPS + 1)
                    if PE_ROWS[b - 1]:
                        act.wait_ge(diag_ready, diags_before(b))
                nc.scalar.activation(wgt[:], hid[:], ACT.Gelu).then_inc(gelu_ready, 1)

            def diagonals(b):
                act.wait_ge(weights_ready, b + 1)
                with act.Fori(0, GROUPS) as i:
                    for m, r in enumerate(PE_ROWS[b]):
                        act.wait_ge(slot_used[r], i + (2 * b + 1) * GROUPS + 1)
                        nc.scalar.sem_inc(diag_tick, 1)
                        nc.scalar.activation(diag[:, m, :], ident[:], ACT.Copy,
                                             scale=wgt[:, bass.ds(i * RING + r, 1)]).then_inc(diag_ready, 1)

            project(0, WAVES[0])
            act.wait_ge(lam_dots_ready, 1)
            nc.scalar.activation(lam[:, 2:4], lam[:, 0:2], ACT.Exp).then_inc(lam_exp_ready, 1)
            attention(0, 0)
            token_to_psum(0)
            query(0, WAVES[0])
            project(1, WAVES[1])
            attention(1, 1)
            gelu(0)
            token_to_psum(1)
            attention(1, 2)
            attention(1, 3)
            query(1, WAVES[1])
            for b in range(1, NB):
                gelu(b)
                if b + 1 < NB:
                    token_to_psum(b + 1)
                diagonals(b)

        @block.vector
        def _(dve):
            steps = [0]

            def link(ins):
                steps[0] += 1
                ins.then_inc(dve_step, 1)
                dve.wait_ge(dve_step, steps[0])

            def links(made):
                for ins in made:
                    steps[0] += 1
                    ins.then_inc(dve_step, 1)
                dve.wait_ge(dve_step, steps[0])

            TT = nc.vector.tensor_tensor
            TS = nc.vector.tensor_scalar
            STT = nc.vector.scalar_tensor_tensor

            def per_half(lo, hi, rows, one):
                if hi - lo >= 8 and (hi - lo) % 4 == 0 and lo % 2 == 0:
                    with dve.Fori(0, (hi - lo) // 4) as i:
                        for g in range(2):
                            for r in rows:
                                one(i * 2 + (lo // 2 + g), r)
                else:
                    for k in range(lo, hi):
                        for r in rows:
                            if r // (RING // 2) == k % 2:
                                one(k // 2, r)

            def dots(b, lo, hi):
                def one(i, r):
                    dve.wait_ge(row_landed[r], i * 16 + 16 * (2 * b * GROUPS + 1))
                    STT(out=ring[:, r, :], in0=ring[:, r, :], scalar=1.0, in1=X[:], op0=ALU.mult, op1=ALU.mult,
                        accum_out=hid[:, bass.ds(i * RING + r, 1)]).then_inc(slot_used[r], 1)
                if lo == 0:
                    dve.wait_ge(token_in_psum, b + 1)
                per_half(lo, hi, range(RING), one)

            def sums(b, lo, hi):
                rows = dve_rows(b)
                before = GROUPS * sum(len(dve_rows(i)) for i in range(b))

                def one(i, r):
                    m = rows.index(r)
                    g = i + (2 * b + 1) * GROUPS
                    w = wgt[:, bass.ds(i * RING + r, 1)]
                    dve.wait_ge(row_landed[r], g * 16 + 16)
                    if b or m or not (isinstance(i, int) and i == 0):
                        dve.wait_ge(low_added, i * len(rows) + m + before)
                    STT(out=xs[:, b, 0:HW], in0=ring[:, r, 0:HW], scalar=w, in1=xs[:, b, 0:HW],
                        op0=ALU.mult, op1=ALU.add).then_inc(low_added, 1)
                    dve.wait_ge(slot_used[rows[m - 1]], g + 2 if m else g + 1)
                    STT(out=xs[:, b, HW:D], in0=ring[:, r, HW:D], scalar=w, in1=xs[:, b, HW:D],
                        op0=ALU.mult, op1=ALU.add).then_inc(slot_used[r], 1)
                per_half(lo, hi, rows, one)

            def weights(b):
                dve.wait_ge(gate_exp_ready, b + 1)
                g = gexp[:].rearrange("p (h k) -> p h k", h=PH)
                link(nc.vector.reduce_sum(gsum[:], g, AX.X))
                link(nc.vector.reciprocal(gsum[:], gsum[:]))
                link(TT(out=g, in0=g, in1=gsum[:].unsqueeze(2).to_broadcast([P, PH, TOPK]), op=ALU.mult))
                link(TS(xs[:, b, :], xs[:, b, :], ALPHA, None, ALU.mult))
                dve.wait_ge(gelu_ready, b + 1)
                TT(out=wgt[:], in0=wgt[:], in1=gexp[:], op=ALU.mult).then_inc(weights_ready, 1)
                dve.wait_ge(weights_ready, b + 1)

            def inverse_root(n):
                v, y, t = rstd[:, 0:n], root[:, 0, 0:n], root[:, 1, 0:n]
                link(TS(t.bitcast(i32), v.bitcast(i32), 1, None, ALU.arith_shift_right))
                link(TS(y.bitcast(i32), t.bitcast(i32), -1.0, float(0x5F3759DF), ALU.mult, ALU.add))
                for step in range(3):
                    link(STT(out=t, in0=y, scalar=-0.5, in1=y, op0=ALU.mult, op1=ALU.mult))
                    link(TT(out=t, in0=t, in1=v, op=ALU.mult))
                    link(STT(out=v if step == 2 else y, in0=t, scalar=1.5, in1=y, op0=ALU.add, op1=ALU.mult))

            def normalise(b, src, gain_bias):
                links([nc.vector.bn_stats(st[:, half, :], src[:, half * HW:(half + 1) * HW]) for half in range(2)])
                link(nc.vector.bn_aggr(mv[:, 0, :], st[:, 0:2, :].rearrange("p a b -> p (a b)")))
                link(TS(rstd[:, 0:1], mv[:, 0, 1:2], EPS, None, ALU.add))
                inverse_root(1)
                link(TS(xs[:, b, :], src, mv[:, 0, 0:1], rstd[:, 0:1], ALU.subtract, ALU.mult))
                link(TT(out=xs[:, b, :], in0=xs[:, b, :], in1=gain_bias[:, 0, :], op=ALU.mult))
                return TT(out=xs[:, b, :], in0=xs[:, b, :], in1=gain_bias[:, 1, :], op=ALU.add)

            def join_sums(b):
                for r in (dve_rows(b)[-1], *PE_ROWS[b][-1:]):
                    dve.wait_ge(slot_used[r], (2 * b + 2) * GROUPS + 1)
                if PE_ROWS[b]:
                    TT(out=xs[:, b, :], in0=xs[:, b, :], in1=ACC[:], op=ALU.add).then_inc(sum_read, 1)
                    dve.wait_ge(sum_read, sum(bool(PE_ROWS[i]) for i in range(b + 1)))

            def finish(b):
                dve.wait_ge(ln2_landed, 32)
                normalise(b, xs[:, b, :], lng).then_inc(block_done, 1)

            proj = [f for f in enumerate(FILLS)]

            def rotary(n):
                b = FILLS[n][2]
                src = W[:, n % 3, :].rearrange("p (h n) -> p h n", h=H)
                a = work[:, 0:HW].rearrange("p (h n) -> p h n", h=H)
                t = work[:, HW:2 * HW].rearrange("p (h n) -> p h n", h=H)
                cos = rp[:, 0, b, :].unsqueeze(1).to_broadcast([P, H, 64])
                sin = rp[:, 1, b, :].unsqueeze(1).to_broadcast([P, H, 64])
                dve.wait_ge(proj_ready, n + 1)
                if rots(n):
                    dve.wait_ge(rot_turned, rots(n))
                links([TT(out=a[:, :, 0:64], in0=src[:, :, 0:64], in1=cos, op=ALU.mult),
                       TT(out=a[:, :, 64:P], in0=src[:, :, 64:P], in1=cos, op=ALU.mult),
                       TT(out=t[:, :, 0:64], in0=src[:, :, 64:P], in1=sin, op=ALU.mult)])
                TT(out=t[:, :, 64:P], in0=src[:, :, 0:64], in1=sin, op=ALU.mult).then_inc(proj_taken_dve, 1)
                dve.wait_ge(proj_taken_dve, takes(n + 1, "dve"))
                link(TT(out=a[:, :, 0:64], in0=a[:, :, 0:64], in1=t[:, :, 0:64], op=ALU.subtract))
                TT(out=a[:, :, 64:P], in0=a[:, :, 64:P], in1=t[:, :, 64:P], op=ALU.add).then_inc(rot_ready, 1)

            def swish_gate(n):
                w, b = FILLS[n][0], FILLS[n][2]
                dve.wait_ge(tanh_ready, gates(n) + 1)
                STT(out=swish[:, b - WAVES[w][0], :], in0=work[:, HW:2 * HW], scalar=1.0, in1=W[:, n % 3, :],
                    op0=ALU.add, op1=ALU.mult).then_inc(proj_taken_dve, 1)

            def fills_of(w, g):
                return [n for n, f in enumerate(FILLS) if f[0] == w and f[1] == g]

            def decay_scores(b):
                for jb in range(b + 1):
                    off = b - jb
                    dve.wait_ge(ret_scored, tiles_before(b) + jb + 1)
                    if off < 2:
                        TT(out=sT[:, jb, :], in0=W[:, jb % 2, :], in1=dec[:, off, :], op=ALU.mult).then_inc(ret_decayed, 1)
                    else:
                        for h in range(H):
                            ins = STT(out=sT[:, jb, h * P:(h + 1) * P], in0=W[:, jb % 2, h * P:(h + 1) * P],
                                      scalar=decay_far[h] ** (off - 1), in1=dec[:, 1, h * P:(h + 1) * P],
                                      op0=ALU.mult, op1=ALU.mult)
                        ins.then_inc(ret_decayed, 1)

            def retention_norm(w, b):
                dve.wait_ge(ret_mixed, b + 1)
                links([nc.vector.bn_stats(st[:, h, :], W[:, 2, h * P:(h + 1) * P]) for h in range(H)])
                links([nc.vector.bn_aggr(mv[:, h, :], st[:, h, :]) for h in range(H)])
                link(TS(rstd[:], mv[:, :, 1], EPS, None, ALU.add))
                inverse_root(H)
                for h in range(H):
                    ins = TS(work[:, h * P:(h + 1) * P], W[:, 2, h * P:(h + 1) * P], mv[:, h, 0:1], rstd[:, h:h + 1],
                             ALU.subtract, ALU.mult)
                    if h == H - 1:
                        ins.then_inc(ret_normed, 1)
                dve.wait_ge(ret_normed, b + 1)
                link(TT(out=work[:, 0:HW], in0=work[:, 0:HW], in1=gn[:, 0, :], op=ALU.mult))
                link(TT(out=work[:, 0:HW], in0=work[:, 0:HW], in1=gn[:, 1, :], op=ALU.add))
                link(TT(out=work[:, 0:HW], in0=work[:, 0:HW], in1=swish[:, b - WAVES[w][0], :], op=ALU.mult))

            def softmax_max(b, h):
                keys_n = (b + 1) * P
                dve.wait_ge(diff_scored, H * b + h + 1)
                link(TT(out=W[:, 0:2, b * P:keys_n], in0=W[:, 0:2, b * P:keys_n],
                        in1=mask[:].unsqueeze(1).to_broadcast([P, 2, P]), op=ALU.add))
                link(nc.vector.reduce_max(smax[:], W[:, 0:2, 0:keys_n], AX.X))
                TS(nmax[:], smax[:], -DK ** -0.5, None, ALU.mult).then_inc(max_ready, 1)

            def softmax_join(b, h):
                keys_n = (b + 1) * P
                dve.wait_ge(exps_ready, H * b + h + 1)
                link(nc.vector.reciprocal(rz[:], zsum[:]))
                link(TS(rz[:, 1:2], rz[:, 1:2], lam[:, 0:1], None, ALU.mult))
                link(TS(probs[:, 1, 0:keys_n], probs[:, 1, 0:keys_n], rz[:, 1:2], None, ALU.mult))
                STT(out=probs[:, 0, 0:keys_n], in0=probs[:, 0, 0:keys_n], scalar=rz[:, 0:1], in1=probs[:, 1, 0:keys_n],
                    op0=ALU.mult, op1=ALU.add).then_inc(a_ready, 1)

            def diff_norm(b):
                dve.wait_ge(squares_ready, b + 1)
                link(TS(rstd[:], ssq[:], 1.0 / P, EPS, ALU.mult, ALU.add))
                inverse_root(H)
                for h in range(H):
                    ins = STT(out=work[:, HW + h * P:HW + (h + 1) * P], in0=W[:, 2, h * P:(h + 1) * P],
                              scalar=rstd[:, h:h + 1], in1=gn[:, 2, h * P:(h + 1) * P], op0=ALU.mult, op1=ALU.mult)
                ins.then_inc(mix_ready, 1)

            def ln1(b):
                if b == 1:
                    dve.wait_ge(x_rest_landed, 16)
                dve.wait_ge(mixer_ready, 2 * (b + 1))
                link(STT(out=xs[:, b, :], in0=xs[:, b, :], scalar=ALPHA, in1=W[:, 2:4, :].rearrange("p a n -> p (a n)"),
                         op0=ALU.mult, op1=ALU.add))
                normalise(b, xs[:, b, :], lng).then_inc(x1_ready, 1)

            def retrieve(b, s):
                best_keys(b, s)
                best_experts(b, s)

            def best_keys(b, s):
                dve.wait_ge(scores_stored, 4 + 3 * s + b if b else s + 1)
                sc = [scores[b][:, s * HW + i * P:s * HW + (i + 1) * P] for i in range(4)]
                left = [cand[:, i * P:(i + 1) * P] for i in range(4)]
                links([nc.vector.max(best_v[:, i, 0:8], sc[i]) for i in range(4)])
                links([nc.vector.match_replace(left[i], best_v[:, i, 0:8], sc[i], LOWEST) for i in range(4)])
                links([nc.vector.max_index(best_i[:, i, 0:8], best_v[:, i, 0:8], sc[i]) for i in range(4)]
                      + [nc.vector.max(best_v[:, i, 8:16], left[i]) for i in range(4)])
                links([nc.vector.max_index(best_i[:, i, 8:16], best_v[:, i, 8:16], left[i]) for i in range(4)])

            def best_experts(b, s):
                v = best_v[:].rearrange("p (h c) k -> p h c k", c=2)
                link(TT(out=cand[:].rearrange("p (h a b) -> p h a b", h=2, a=TOPK),
                        in0=v[:, :, 0, :].unsqueeze(3).to_broadcast([P, 2, TOPK, TOPK]),
                        in1=v[:, :, 1, :].unsqueeze(2).to_broadcast([P, 2, TOPK, TOPK]), op=ALU.add))
                c = [cand[:, h * 256:(h + 1) * 256] for h in range(2)]
                tp = [top_p[:, h * TOPK:(h + 1) * TOPK] for h in range(2)]
                links([nc.vector.max(top_v[:, h, 0:8], c[h]) for h in range(2)])
                links([nc.vector.max_index(tp[h][:, 0:8], top_v[:, h, 0:8], c[h]) for h in range(2)])
                links([nc.vector.match_replace(c[h], top_v[:, h, 0:8], c[h], LOWEST) for h in range(2)])
                links([nc.vector.max(top_v[:, h, 8:16], c[h]) for h in range(2)])
                links([nc.vector.max_index(tp[h][:, 8:16], top_v[:, h, 8:16], c[h]) for h in range(2)])
                link(nc.vector.tensor_copy(half_f[:], best_i[:]))
                i_f = half_f[:].rearrange("p (h c) k -> p h c k", c=2)
                onehot = cand[:].rearrange("p (e a) -> p e a", a=TOPK)
                pick = cand[:].rearrange("p (h k a) -> p h k a", h=2, k=TOPK)
                n = 2 * TOPK
                halves = ((ALU.logical_shift_right, 4), (ALU.bitwise_and, 15))
                links([TS(pos_u[:, c, :], top_p[:], arg, None, op) for c, (op, arg) in enumerate(halves)])
                link(nc.vector.tensor_copy(pos_f[:], pos_u[:]))
                for c in range(2):
                    link(TT(out=onehot, in0=pos_f[:, c, :].unsqueeze(2).to_broadcast([P, n, TOPK]),
                            in1=iota_f[:].unsqueeze(1).to_broadcast([P, n, TOPK]), op=ALU.is_equal))
                    link(TT(out=pick, in0=pick, in1=i_f[:, :, c, :].unsqueeze(2).to_broadcast([P, 2, TOPK, TOPK]),
                            op=ALU.mult))
                    link(nc.vector.reduce_sum(sel[:, c, :], onehot, AX.X))
                link(TT(out=gate[:, b, s * n:(s + 1) * n].rearrange("p (h k) -> p h k", h=2), in0=top_v[:],
                        in1=top_v[:, :, 0:1].to_broadcast([P, 2, TOPK]), op=ALU.subtract))
                STT(out=idx[:, b, s * n:(s + 1) * n], in0=sel[:, 0, :], scalar=float(P), in1=sel[:, 1, :],
                    op0=ALU.mult, op1=ALU.add).then_inc(experts_ready, 1)

            dve.wait_ge(iota_ready, 1)
            link(nc.vector.tensor_copy(iota_f[:], iota_i[:]))
            dve.wait_ge(rope_landed, 32)

            rotary(fills_of(0, RQ)[0])
            rotary(fills_of(0, RK)[0])
            swish_gate(fills_of(0, RG)[0])
            dve.wait_ge(lam_landed, 64)
            lam_v = lam_in[:].rearrange("p (a b) n -> p a b n", b=2)
            link(TT(out=lam_v[:, :, 0, :], in0=lam_v[:, :, 0, :], in1=lam_v[:, :, 1, :], op=ALU.mult))
            nc.vector.reduce_sum(lam[:, 0:2], lam_v[:, :, 0, :], AX.X).then_inc(lam_dots_ready, 1)
            dve.wait_ge(tabs_landed, 5 * 16)
            link(TS(gn[:, 0:2, :], gn[:, 0:2, :], 0.5, None, ALU.mult))
            link(TS(gn[:, 2, :], gn[:, 2, :], 1.0 - LAMBDA_INIT, None, ALU.mult))
            dve.wait_ge(lam_exp_ready, 1)
            link(TT(out=lam[:, 1:2], in0=lam[:, 3:4], in1=lam[:, 2:3], op=ALU.subtract))
            link(TS(lam[:, 0:1], lam[:, 1:2], -LAMBDA_INIT, None, ALU.add))
            decay_scores(0)
            retention_norm(0, 0)
            for h in range(H):
                softmax_max(0, h)
                softmax_join(0, h)
            diff_norm(0)
            dve.wait_ge(x_landed, 16)
            dve.wait_ge(ln1_landed, 32)
            ln1(0)
            retrieve(0, 0)
            retrieve(0, 1)
            dots(0, 0, 2)
            retrieve(0, 2)
            turned = fills_of(1, RQ) + fills_of(1, RK)
            rotary(turned[0])
            dots(0, 2, 3)
            retrieve(0, 3)
            k = 3
            for n in turned[1:]:
                rotary(n)
                dots(0, k, k + 1)
                k += 1
            for n in fills_of(1, RG):
                dots(0, k, k + 2)
                swish_gate(n)
                k += 2
            dots(0, k, 22)
            decay_scores(1)
            dots(0, 22, 23)
            retention_norm(1, 1)
            k = 23
            for h in range(H):
                softmax_max(1, h)
                dots(0, k, k + 1)
                softmax_join(1, h)
                k += 1
            diff_norm(1)
            dots(0, k, 30)
            dots(0, 30, 32)
            ln1(1)
            weights(0)
            k = 0
            for b in (2, 3):
                decay_scores(b)
                sums(0, k, k + 1)
                retention_norm(1, b)
                k += 1
                for h in range(H):
                    softmax_max(b, h)
                    sums(0, k, k + 1)
                    softmax_join(b, h)
                    k += 1
                diff_norm(b)
                sums(0, k, k + 3)
                k += 3
                ln1(b)
            sums(0, k, 20)
            best_keys(1, 0)
            sums(0, 20, 22)
            best_experts(1, 0)
            sums(0, 22, 32)

            dots(1, 0, 1)
            join_sums(0)
            dots(1, 1, 4)
            for s in range(1, 4):
                best_keys(1, s)
                dots(1, 8 * s - 4, 8 * s - 2)
                best_experts(1, s)
                dots(1, 8 * s - 2, 8 * s + 4)
            dots(1, 28, 32)
            for b in range(1, NB):
                weights(b)
                sums(b, 0, 2)
                if b == 1:
                    finish(0)
                sums(b, 2, 4)
                for s in range(4):
                    if b + 1 < NB:
                        best_keys(b + 1, s)
                        sums(b, 4 + 7 * s, 7 + 7 * s)
                        best_experts(b + 1, s)
                        sums(b, 7 + 7 * s, 11 + 7 * s)
                    else:
                        sums(b, 4 + 7 * s, 11 + 7 * s)
                if b + 1 < NB:
                    dots(b + 1, 0, 1)
                join_sums(b)
                if b + 1 < NB:
                    dots(b + 1, 1, 4)
                if b:
                    finish(b)
                if b + 1 < NB:
                    dots(b + 1, 4, 32)


def constants():
    import numpy as np
    log_g = np.log1p(-(2.0 ** (-5.0 - np.arange(H))))
    i = np.arange(P)
    rel = (i[None, :] - i[:, None])[:, None, :]
    near = np.where(rel >= 0, np.exp(np.maximum(rel, 0) * log_g[None, :, None]), 0.0)
    far = np.exp((rel + P) * log_g[None, :, None])
    decay = (np.stack([near, far], axis=1) * P ** -0.5).reshape(P, 2, HW)
    ang = np.arange(S)[:, None] * (10000.0 ** (-np.arange(64) / 64.0))[None, :]
    rope = np.stack([np.cos(ang), np.sin(ang)])
    mask = np.where(i[None, :] > i[:, None], MASKED, 0.0)
    f = np.float32
    return {"decay": decay.astype(f), "rope": rope.astype(f), "ident_in": np.eye(P, dtype=f),
            "mask_in": mask.astype(f)}, [float(v) for v in np.exp(P * log_g)]


INPUTS = ["x", "xT", "w_in", "ret_gn_g", "ret_gn_b", "diff_lambda_q1", "diff_lambda_k1", "diff_lambda_q2",
          "diff_lambda_k2", "diff_subln_g", "w_out", "ln1_g", "ln1_b", "peer_w_query", "keysT", "peer_u",
          "peer_v", "ln2_g", "ln2_b", "decay", "rope", "ident_in", "mask_in"]


def kernel(**inputs):
    import numpy as np
    import concourse.bacc as bacc
    from concourse.bass_utils import run_bass_kernel_spmd

    given = {n: np.asarray(a)[0] for n, a in inputs.items()}
    given["xT"] = given["x"].T
    given["keysT"] = given["peer_sub_keys"].transpose(3, 0, 1, 2).reshape(P, HC, P)
    tables, decay_far = constants()
    given.update(tables)
    nc = bacc.Bacc("TRN2", target_bir_lowering=False, num_devices=1)
    arrays, aps = {}, []
    for name in INPUTS:
        a = np.ascontiguousarray(given[name])
        arrays[name] = a
        aps.append(nc.dram_tensor(name, a.shape, mybir.dt.from_np(a.dtype), kind="ExternalInput").ap())
    out = nc.dram_tensor("out", (S, D), fp32, kind="ExternalOutput").ap()
    build(nc, *aps, decay_far, out)
    r = run_bass_kernel_spmd(nc, [arrays], core_ids=[0])
    return r.results[0]["out"].reshape(1, S, D)
```

```python
import concourse.bass as bass
from concourse import mybir
from contextlib import ExitStack

fp32 = mybir.dt.float32
i32 = mybir.dt.int32
u32 = mybir.dt.uint32
ALU = mybir.AluOpType
ACT = mybir.ActivationFunctionType
AX = mybir.AxisListType

P = 128
S = 512
D = 1024
KD = D // P
NB = S // P
H = 4
HW = 512
DK = 64
HC = 16
PH = 8
TOPK = 16
E = PH * TOPK
ALPHA = 2.0 ** 0.25
LAMBDA_INIT = 0.8 - 0.6
EPS = 1e-5
LOWEST = -3.0e38
MASKED = -1.0e30
WAVES = [[0], [1, 2, 3]]
NW = 2
RING = 8
HALF = RING // 2
LAG = 40
U_GROUPS = E // RING
V_GROUPS = (E - LAG) // RING
MIXED = (NB - 1) * E // HALF
TAIL = LAG // RING
AT_V, AT_MIXED = U_GROUPS, U_GROUPS + V_GROUPS
AT_TAIL = AT_MIXED + MIXED
BESIDE_MIXER = [1, 1, 2, 2, 1, 1, 2]
BESIDE_QUERY = [0] * 13 + [1, 1, 2]
SHARED = sum(BESIDE_MIXER) // 2
PE_BESIDE = sum(BESIDE_QUERY) // 2
QUARTER = E // 4
PERIOD = QUARTER // HALF
PE_SLOTS = [3, 5, 7]
DVE_SLOT = 1
DVE_SLOTS = [r for r in range(RING) if r not in PE_SLOTS]
RQ, RK, RV, RG, DQ, DKK, DV = range(7)
WIN, WOUT, WQ = 7, 2, 4
PER_WAVE = WIN + WOUT + WQ


def proj_fills():
    out = []
    for w, blocks in enumerate(WAVES):
        for g in range(WIN):
            if g in (DQ, DKK):
                out += [(w, g, h, "act") for h in (range(H) if w else [None])]
            else:
                out += [(w, g, b, "dve" if g in (RQ, RK, RG) else "act") for b in blocks]
    return out


FILLS = proj_fills()


def takes(n, who):
    return sum(f[3] == who for f in FILLS[:n])


def rots(n):
    return sum(f[1] in (RQ, RK) for f in FILLS[:n])


def gates(n):
    return sum(f[1] == RG for f in FILLS[:n])


def tiles_before(b):
    return b * (b + 1) // 2


def beside_mixer(b, step):
    before = sum(BESIDE_MIXER[:step])
    return range(before, before + BESIDE_MIXER[step]) if b == NB - 1 else []


def beside_query(t):
    before = 2 * V_GROUPS + sum(BESIDE_QUERY[:t])
    return range(before, before + BESIDE_QUERY[t])


def pe_slots(k):
    return [r for r in PE_SLOTS if r // HALF == k % 2 and not SHARED <= k // 2 < V_GROUPS]


def diags_before(n):
    return len(PE_SLOTS) * (min(n - AT_V, SHARED) + max(n - AT_MIXED, 0))


def dve_slots(i):
    return DVE_SLOTS if i < SHARED else list(range(RING))


def turn_of(b):
    return (b * E - (E - LAG)) // HALF


def build(nc, x, xT, w_in, ret_gn_g, ret_gn_b, lq1, lk1, lq2, lk2, subln_g, w_out, ln1_g, ln1_b,
          w_query, keysT, peer_u, peer_v, ln2_g, ln2_b, decay, rope, ident_in, mask_in, decay_far, out):
    ctx = ExitStack()
    with ctx:
        def sb(name, shape, dt=fp32):
            return ctx.enter_context(nc.sbuf_tensor(name, shape, dt))

        def sem(name):
            return ctx.enter_context(nc.semaphore(name))

        wt = sb("wt", [P, NW, KD, HW])
        actT = sb("actT", [P, KD, S])
        xs = sb("xs", [P, NB, D])
        qT = sb("qT", [P, H, 3 * P])
        kT = sb("kT", [P, H, S])
        rv = sb("rv", [P, NB, HW])
        swish = sb("swish", [P, 3, HW])
        dqT = sb("dqT", [P, H, 3 * P])
        dkT = sb("dkT", [P, H, S])
        dv = sb("dv", [P, NB, HW])
        keys = sb("keys", [P, HC, P])
        dec = sb("dec", [P, 2, HW])
        rp = sb("rp", [P, 2, NB, 64])
        lng = sb("lng", [P, 2, D])
        gn = sb("gn", [P, 3, HW])
        ident = sb("ident", [P, P])
        mask = sb("mask", [P, P])
        ring = sb("ring", [P, RING, D])
        attn = sb("attn", [P, 3 * HW])
        probs = attn[:, 0:2 * HW].rearrange("p (c n) -> p c n", c=2)
        aT = attn[:, 2 * HW:3 * HW]
        qq = attn[:, :].rearrange("p (i t) -> p i t", i=4)
        wide = sb("wide", [P, 4 * HW])
        sT = wide[:, :].rearrange("p (j n) -> p j n", j=NB)
        mixT = wide[:, 0:D].rearrange("p (k t) -> p k t", k=KD)
        work = sb("work", [P, 2 * HW])
        best_v = sb("best_v", [P, 4, TOPK])
        best_i = sb("best_i", [P, 4, TOPK], u32)
        cand = sb("cand", [P, 2 * TOPK * TOPK])
        top_v = sb("top_v", [P, 2, TOPK])
        top_p = sb("top_p", [P, 2 * TOPK], u32)
        half_f = sb("half_f", [P, 4, TOPK])
        pos_u = sb("pos_u", [P, 2, 2 * TOPK], u32)
        pos_f = sb("pos_f", [P, 2, 2 * TOPK])
        sel = sb("sel", [P, 2, 2 * TOPK])
        iota_i = sb("iota_i", [P, TOPK], i32)
        iota_f = sb("iota_f", [P, TOPK])
        idx = sb("idx", [P, NB * E], i32)
        gate = sb("gate", [P, NB * E])
        diag = sb("diag", [P, 2, len(PE_SLOTS), P])
        stage = sb("stage", [P, 2, RING], i32)
        hid = sb("hid", [P, NB * E])
        st = sb("st", [P, 4, 6])
        mv = sb("mv", [P, 4, 2])
        rstd = sb("rstd", [P, 4])
        root = sb("root", [P, 2, 4])
        smax = sb("smax", [P, 2 * H])
        nmax = sb("nmax", [P, 2 * H])
        zsum = sb("zsum", [P, 2 * H])
        rz = sb("rz", [P, 2 * H])
        ssq = sb("ssq", [P, 4])
        lam_in = sb("lam_in", [P, 4, DK])
        lam = sb("lam", [P, 4])
        gsum = sb("gsum", [P, PH])

        scores = {0: wide[:], 1: rv[:].rearrange("p b n -> p (b n)"), 2: kT[:].rearrange("p h n -> p (h n)"),
                  3: dkT[:].rearrange("p h n -> p (h n)")}

        W = ctx.enter_context(nc.psum_tensor("W", [P, 4, HW], fp32))
        X = ctx.enter_context(nc.psum_tensor("X", [P, D], fp32))
        ACC = ctx.enter_context(nc.psum_tensor("ACC", [P, D], fp32))

        def out_banks(b, ph):
            if b == 0:
                return [W[:, 2 * ph + half, :] for half in range(2)]
            Y = ACC if b == 1 else X
            return [Y[:, half * HW:(half + 1) * HW] for half in range(2)]

        w_landed = [sem(f"w_landed{i}") for i in range(NW)]
        xT_landed = sem("xT_landed")
        xT_rest_landed = sem("xT_rest_landed")
        x_landed = sem("x_landed")
        x_rest_landed = sem("x_rest_landed")
        rope_landed = sem("rope_landed")
        tabs_landed = sem("tabs_landed")
        lam_landed = sem("lam_landed")
        ln1_landed = sem("ln1_landed")
        ln2_landed = sem("ln2_landed")
        keys_landed = sem("keys_landed")
        row_landed = [sem(f"row_landed{i}") for i in range(RING)]
        stored = sem("stored")
        proj_ready = sem("proj_ready")
        rot_turned = sem("rot_turned")
        ret_scored = sem("ret_scored")
        ret_mixed = sem("ret_mixed")
        diff_scored = sem("diff_scored")
        a_turned = sem("a_turned")
        diff_mixed = sem("diff_mixed")
        mix_turned = sem("mix_turned")
        mixer_ready = sem("mixer_ready")
        x1_turned = sem("x1_turned")
        query_ready = sem("query_ready")
        keys_scored = sem("keys_scored")
        proj_taken_act = sem("proj_taken_act")
        tanh_ready = sem("tanh_ready")
        rot_taken = sem("rot_taken")
        exps_ready = sem("exps_ready")
        a_taken = sem("a_taken")
        squares_ready = sem("squares_ready")
        mix_taken = sem("mix_taken")
        x1_taken = sem("x1_taken")
        query_taken = sem("query_taken")
        token_in_psum = sem("token_in_psum")
        gelu_ready = sem("gelu_ready")
        gate_exp_ready = sem("gate_exp_ready")
        scores_stored = sem("scores_stored")
        diag_ready = sem("diag_ready")
        lam_exp_ready = sem("lam_exp_ready")
        diag_tick = sem("diag_slot_checked")
        proj_taken_dve = sem("proj_taken_dve")
        rot_ready = sem("rot_ready")
        ret_decayed = sem("ret_decayed")
        ret_normed = sem("ret_normed")
        max_ready = sem("max_ready")
        a_ready = sem("a_ready")
        mix_ready = sem("mix_ready")
        x1_ready = sem("x1_ready")
        experts_ready = sem("experts_ready")
        slot_used = [sem(f"slot_used{i}") for i in range(RING)]
        weights_ready = sem("weights_ready")
        low_added = sem("low_added")
        sum_read = sem("sum_read")
        block_done = sem("block_done")
        lam_dots_ready = sem("lam_dots_ready")
        dve_step = sem("dve_step")
        iota_ready = sem("iota_ready")
        staged = sem("staged")
        staged_tick = sem("slot_checked")

        block = ctx.enter_context(nc.Block())

        def wslot(w, i):
            n = w * PER_WAVE + i
            return n % NW, 16 * (n // NW + 1)

        @block.sync
        def _(sp):
            def wait_used(w, i):
                if i < WIN:
                    sp.wait_ge(proj_ready, sum(f[:2] <= (w, i) for f in FILLS))
                elif i < WIN + WOUT:
                    sp.wait_ge(mixer_ready, 2 * WAVES[w][-1] + i - WIN + 1)
                else:
                    s = i - WIN - WOUT
                    sp.wait_ge(query_ready, (4 + 4 * (s + 1)) if w else s + 1)

            def load_w(w, i):
                n = w * PER_WAVE + i
                if n >= NW:
                    wait_used(*divmod(n - NW, PER_WAVE))
                if i < WIN:
                    src = w_in[:, i * HW:(i + 1) * HW]
                elif i < WIN + WOUT:
                    src = w_out[:, (i - WIN) * HW:(i - WIN + 1) * HW]
                else:
                    j = i - WIN - WOUT
                    src = w_query[:, j * HW:(j + 1) * HW]
                src = src.rearrange("(k p) n -> p k n", p=P)
                sp.dma_start(wt[:, n % NW, :, :], src).then_inc(w_landed[n % NW], 16)

            xT_k = xT.rearrange("(k p) t -> p k t", p=P)
            x_b = x.rearrange("(b p) d -> p b d", p=P)
            sp.dma_start(actT[:, :, 0:P], xT_k[:, :, 0:P]).then_inc(xT_landed, 16)
            load_w(0, 0)
            sp.dma_start(rp[:], rope.rearrange("c (b p) n -> p c b n", p=P)).then_inc(rope_landed, 16)
            sp.dma_start(ident[:], ident_in).then_inc(rope_landed, 16)
            for i in range(1, DQ):
                load_w(0, i)
            sp.dma_start(dec[:], decay).then_inc(tabs_landed, 16)
            for i, v in enumerate((ret_gn_g, ret_gn_b, subln_g)):
                sp.dma_start(gn[:, i, :], v.partition_broadcast(P)).then_inc(tabs_landed, 16)
            sp.dma_start(mask[:], mask_in).then_inc(tabs_landed, 16)
            for i, v in enumerate((lq1, lk1, lq2, lk2)):
                sp.dma_start(lam_in[:, i, :], v.partition_broadcast(P)).then_inc(lam_landed, 16)
            for i in range(DQ, WIN):
                load_w(0, i)
            load_w(0, WIN)
            sp.dma_start(xs[:, 0, :], x_b[:, 0, :]).then_inc(x_landed, 16)
            load_w(0, WIN + 1)
            for i, v in enumerate((ln1_g, ln1_b)):
                sp.dma_start(lng[:, i, :], v.partition_broadcast(P)).then_inc(ln1_landed, 16)
            sp.dma_start(keys[:], keysT).then_inc(keys_landed, 16)
            load_w(0, WIN + WOUT)
            sp.dma_start(actT[:, :, P:S], xT_k[:, :, P:S]).then_inc(xT_rest_landed, 16)
            load_w(0, WIN + WOUT + 1)
            sp.dma_start(xs[:, 1:NB, :], x_b[:, 1:NB, :]).then_inc(x_rest_landed, 16)
            for i in range(WIN + WOUT + 2, PER_WAVE):
                load_w(0, i)
            for i in range(PER_WAVE):
                load_w(1, i)
            sp.wait_ge(x1_ready, NB)
            for i, v in enumerate((ln2_g, ln2_b)):
                sp.dma_start(lng[:, i, :], v.partition_broadcast(P)).then_inc(ln2_landed, 16)
            for b in range(NB):
                sp.wait_ge(block_done, b + 1)
                sp.dma_start(out[b * P:(b + 1) * P, :], xs[:, b, :]).then_inc(stored, 16)
            sp.wait_ge(stored, 16 * NB)

        @block.gpsimd
        def _(pool):
            nc.gpsimd.iota(iota_i[:], pattern=[[1, TOPK]], base=0, channel_multiplier=0).then_inc(iota_ready, 1)
            for r in range(RING):
                nc.gpsimd.sem_inc(slot_used[r], 1)
            def fetch(table, r, half, c, n):
                pool.wait_ge(slot_used[r], n + 1)
                nc.gpsimd.sem_inc(staged_tick, 1)
                pool.indirect_dma_start(
                    out=ring[:, r, :], out_offset=None, in_=table,
                    in_offset=bass.IndirectOffsetOnAxis(ap=stage[:, half, c:c + 1], axis=0),
                ).then_inc(row_landed[r], 16)

            def one_table(table, first, n, half, staged_before):
                nc.gpsimd.tensor_copy(stage[:, half, :], idx[:, bass.ds(first, RING)]).then_inc(staged, 1)
                pool.wait_ge(staged, staged_before + 1)
                for r in range(RING):
                    fetch(table, r, half, r, n)

            def both_tables(first_u, first_v, n, half, staged_before):
                nc.gpsimd.tensor_copy(stage[:, half, 0:HALF], idx[:, bass.ds(first_u, HALF)]).then_inc(staged, 1)
                nc.gpsimd.tensor_copy(stage[:, half, HALF:RING], idx[:, bass.ds(first_v, HALF)]).then_inc(staged, 1)
                pool.wait_ge(staged, staged_before + 2)
                for r in range(RING):
                    fetch(peer_v if r % 2 else peer_u, r, half, r // 2 + HALF * (r % 2), n)

            per = QUARTER // RING
            with pool.Fori(0, 4) as quarter:
                pool.wait_ge(experts_ready, quarter + 1)
                for j in range(per):
                    n = quarter * per + j
                    one_table(peer_u, quarter * QUARTER + j * RING, n, j % 2, n)
            for i in range(V_GROUPS):
                n = AT_V + i
                one_table(peer_v, i * RING, n, n % 2, n)
            with pool.Fori(0, MIXED // PERIOD) as quarter:
                pool.wait_ge(experts_ready, quarter + 5)
                for j in range(PERIOD):
                    both_tables(quarter * QUARTER + (E + j * HALF), quarter * QUARTER + (E - LAG + j * HALF),
                                quarter * PERIOD + (AT_MIXED + j), (AT_MIXED + j) % 2,
                                quarter * (2 * PERIOD) + (AT_MIXED + 2 * j))
            for i in range(TAIL):
                n = AT_TAIL + i
                one_table(peer_v, NB * E - LAG + i * RING, n, n % 2, AT_MIXED + 2 * MIXED + i)

        @block.tensor
        def _(pe):
            fill = [0]

            def add_rows(n, odd, diags, slots=PE_SLOTS, start=False, stop=False):
                for r in slots:
                    m = PE_SLOTS.index(r)
                    pe.wait_ge(row_landed[r], n * 16 + 16)
                    pe.wait_ge(diag_ready, diags + (m + 1))
                    for half in range(2):
                        last = nc.tensor.matmul(
                            ACC[:, half * HW:(half + 1) * HW], diag[:, odd, m, :], ring[:, r, half * HW:(half + 1) * HW],
                            start=start and m == 0, stop=stop and m == len(PE_SLOTS) - 1)
                    last.then_inc(slot_used[r], 1)

            def beside(halves):
                for k in halves:
                    n = AT_V + k // 2
                    add_rows(n, n % 2, diags_before(n), pe_slots(k), start=k < 2)

            def add_block(b):
                lo = AT_MIXED + turn_of(b) if b else AT_MIXED + PE_BESIDE
                hi = AT_MIXED + turn_of(b + 1) if b < NB - 1 else AT_TAIL + TAIL
                made = len(PE_SLOTS)
                if b:
                    pe.wait_ge(sum_read, b)
                    add_rows(lo, lo % 2, diags_before(lo), start=True)
                    lo += 1
                pairs = (hi - lo - 1) // 2
                with pe.Fori(0, pairs) as i:
                    for j in range(2):
                        n = lo + j
                        add_rows(i * 2 + n, n % 2, i * (2 * made) + diags_before(n))
                for n in range(lo + 2 * pairs, hi):
                    add_rows(n, n % 2, diags_before(n), stop=n == hi - 1)

            def turn(n):
                pe.wait_ge(rot_ready, n + 1)
                if n:
                    pe.wait_ge(rot_taken, n)
                for h in range(H):
                    last = nc.tensor.transpose(W[:, 3, h * P:(h + 1) * P], work[:, h * P:(h + 1) * P], ident[:])
                last.then_inc(rot_turned, 1)

            def project(w, blocks):
                toks = slice(blocks[0] * P, (blocks[-1] + 1) * P)
                n_tok = len(blocks) * P
                for g in range(WIN):
                    slot, landed = wslot(w, g)
                    pe.wait_ge(w_landed[slot], landed)
                    wide_tile = g in (DQ, DKK)
                    parts = (range(H) if w else [None]) if wide_tile else blocks
                    for part in parts:
                        n = fill[0]
                        assert FILLS[n][:3] == (w, g, part)
                        if n >= 3:
                            who = FILLS[n - 3][3]
                            pe.wait_ge(proj_taken_act if who == "act" else proj_taken_dve, takes(n - 2, who))
                        bank = W[:, n % 3, :]
                        if not wide_tile:
                            for k in range(KD):
                                last = nc.tensor.matmul(bank, actT[:, k, part * P:(part + 1) * P],
                                                        wt[:, slot, k, :], start=(k == 0), stop=(k == KD - 1))
                        else:
                            for h in (range(H) if part is None else [part]):
                                at = h * P if part is None else 0
                                for k in range(KD):
                                    last = nc.tensor.matmul(bank[:, at:at + n_tok], wt[:, slot, k, h * P:(h + 1) * P],
                                                            actT[:, k, toks], start=(k == 0), stop=(k == KD - 1))
                        last.then_inc(proj_ready, 1)
                        fill[0] += 1
                        if n and FILLS[n - 1][0] == w and FILLS[n - 1][1] in (RQ, RK):
                            turn(rots(n) - 1)
                        if w and g in (DQ, DKK, DV):
                            retention_step(n - fills_before_diff)
                    if w == 0 and g == RG:
                        pe.wait_ge(rot_taken, rots(fill[0]))
                        retention_score(0, 0)
                    elif w == 0 and g == DQ:
                        pe.wait_ge(proj_taken_act, takes(RV + 1, "act"))
                        retention_mix(0)
                    elif w == 0 and g == DKK:
                        pe.wait_ge(proj_taken_act, takes(DKK + 1, "act"))
                        for h in range(H):
                            for c in range(2):
                                last = nc.tensor.matmul(X[:, c * HW + h * P:c * HW + (h + 1) * P],
                                                        dqT[c * DK:(c + 1) * DK, h, 0:P],
                                                        dkT[c * DK:(c + 1) * DK, h, 0:P], start=True, stop=True)
                        last.then_inc(diff_scored, H)

            def diff_0():
                pe.wait_ge(a_ready, H)
                for h in range(H):
                    last = nc.tensor.transpose(ACC[:, HW + h * P:HW + (h + 1) * P], probs[:, 0, h * P:(h + 1) * P], ident[:])
                last.then_inc(a_turned, H)
                pe.wait_ge(a_taken, H)
                pe.wait_ge(proj_taken_act, takes(DV + 1, "act"))
                for h in range(H):
                    last = nc.tensor.matmul(W[:, 2, h * P:(h + 1) * P], aT[:, h * P:(h + 1) * P],
                                            dv[:, 0, h * P:(h + 1) * P], start=True, stop=True)
                last.then_inc(diff_mixed, 1)

            RETENTION = [(1, (0, 1)), (1, None), (2, (0, 1)), (2, (2,)), (2, None), (3, (0, 1)), (3, (2, 3)), (3, None)]
            fills_before_diff = sum((f[0], f[1]) < (1, DQ) for f in FILLS)

            def retention_step(t):
                if t == 0:
                    pe.wait_ge(rot_taken, rots(len(FILLS)))
                    pe.wait_ge(proj_taken_act, takes(fills_before_diff, "act"))
                if 0 < t <= len(RETENTION):
                    b, keys_of = RETENTION[t - 1]
                    if keys_of is None:
                        retention_mix(b)
                    else:
                        for jb in keys_of:
                            retention_score(b, jb)

            def retention_score(b, jb):
                q = b - (b > 0)
                n = tiles_before(b) + jb
                if n > 2:
                    pe.wait_ge(ret_decayed, n - 1)
                for h in range(H):
                    bank = ACC[:, jb % 2 * HW:(jb % 2 + 1) * HW]
                    last = nc.tensor.matmul(bank[:, h * P:(h + 1) * P], kT[:, h, jb * P:(jb + 1) * P],
                                            qT[:, h, q * P:(q + 1) * P], start=True, stop=True)
                last.then_inc(ret_scored, 1)

            def retention_mix(b):
                pe.wait_ge(ret_decayed, tiles_before(b + 1))
                if b > 1:
                    pe.wait_ge(ret_normed, b)
                for h in range(H):
                    for jb in range(b + 1):
                        last = nc.tensor.matmul(W[:, 3, h * P:(h + 1) * P], sT[:, jb, h * P:(h + 1) * P],
                                                rv[:, jb, h * P:(h + 1) * P], start=(jb == 0), stop=(jb == b))
                last.then_inc(ret_mixed, 1)

            def diff(b):
                q = b - 1
                keys_n = (b + 1) * P

                def score(h):
                    if h or b > 1:
                        pe.wait_ge(exps_ready, H * b + h)
                    else:
                        pe.wait_ge(proj_taken_act, takes(fill[0], "act"))
                    for c in range(2):
                        last = nc.tensor.matmul(W[:, c, 0:keys_n], dqT[c * DK:(c + 1) * DK, h, q * P:(q + 1) * P],
                                                dkT[c * DK:(c + 1) * DK, h, 0:keys_n], start=True, stop=True)
                    last.then_inc(diff_scored, 1)

                score(0)
                for h in range(H):
                    if h < H - 1:
                        score(h + 1)
                    if b > 1 and h == 0:
                        turn_mixed(b - 1)
                    elif b > 1 and h < 3:
                        out_half(b - 1, h - 1)
                    beside(beside_mixer(b, h))
                    n = H * b + h
                    pe.wait_ge(a_ready, n + 1)
                    if b == 1 and h == 0:
                        pe.wait_ge(ret_normed, NB)
                    else:
                        pe.wait_ge(a_taken, n)
                    for kb in range(b + 1):
                        last = nc.tensor.transpose(W[:, 3, kb * P:(kb + 1) * P], probs[:, 0, kb * P:(kb + 1) * P], ident[:])
                    last.then_inc(a_turned, 1)
                    pe.wait_ge(a_taken, n + 1)
                    if h == 0 and b > 1:
                        pe.wait_ge(mix_ready, b)
                    for kb in range(b + 1):
                        last = nc.tensor.matmul(W[:, 2, h * P:(h + 1) * P], aT[:, kb * P:(kb + 1) * P],
                                                dv[:, kb, h * P:(h + 1) * P], start=(kb == 0), stop=(kb == b))
                last.then_inc(diff_mixed, 1)

            def turn_mixed(b):
                pe.wait_ge(mix_ready, b + 1)
                if b == 1:
                    pe.wait_ge(ret_decayed, tiles_before(NB))
                elif b == 2:
                    pe.wait_ge(slot_used[RING - 1], U_GROUPS + 1)
                elif b == 3:
                    pe.wait_ge(x1_taken, 2 * b)
                q = b - (b > 0)
                for half in range(2):
                    for k in range(4):
                        src = swish[:, q, :] if half == 0 else work[:, HW:2 * HW]
                        dst = out_banks(b, 0)[half]
                        last = nc.tensor.transpose(dst[:, k * P:(k + 1) * P], src[:, k * P:(k + 1) * P], ident[:])
                    last.then_inc(mix_turned, 1)

            def out_half(b, half):
                pe.wait_ge(mix_taken, 2 * (b + 1))
                slot, landed = wslot(int(b > 0), WIN + half)
                pe.wait_ge(w_landed[slot], landed)
                for k in range(KD):
                    last = nc.tensor.matmul(out_banks(b, 1)[half], mixT[:, k, :], wt[:, slot, k, :],
                                            start=(k == 0), stop=(k == KD - 1))
                last.then_inc(mixer_ready, 1)

            def turn_x1(b):
                pe.wait_ge(x1_ready, b + 1)
                for half in range(2):
                    for k in range(4):
                        c = 4 * half + k
                        last = nc.tensor.transpose(out_banks(b, 0)[half][:, k * P:(k + 1) * P],
                                                   xs[:, b, c * P:(c + 1) * P], ident[:])
                    last.then_inc(x1_turned, 1)

            def query(w, blocks):
                n_tok = len(blocks) * P
                toks = slice(blocks[0] * P, (blocks[-1] + 1) * P)
                pe.wait_ge(x1_taken, 2 * (blocks[-1] + 1))
                pe.wait_ge(keys_landed, 16)
                fq = 16 if w else 4
                for s in range(WQ):
                    slot, landed = wslot(w, WIN + WOUT + s)
                    pe.wait_ge(w_landed[slot], landed)
                    for i in range(4):
                        n = (4 + 4 * s + i) if w else s
                        if (w or i == 0) and n - (4 if w else 0) >= 2:
                            pe.wait_ge(query_taken, n - 1)
                        dst = W[:, 2 + n % 2, 0:n_tok] if w else W[:, 2 + n % 2, i * P:(i + 1) * P]
                        for k in range(KD):
                            last = nc.tensor.matmul(dst, wt[:, slot, k, i * P:(i + 1) * P], actT[:, k, toks],
                                                    start=(k == 0), stop=(k == KD - 1))
                        if w or i == 3:
                            last.then_inc(query_ready, 1)
                        if w and i < 3:
                            beside(beside_query(4 * s + i))
                    pe.wait_ge(query_taken, (4 + 4 * (s + 1)) if w else s + 1)
                    for j in range(len(blocks)):
                        n = (4 if w else 0) + s * len(blocks) + j
                        if n - (4 if w else 0) >= 2:
                            pe.wait_ge(scores_stored, n - 1)
                        for i in range(4):
                            last = nc.tensor.matmul(W[:, n % 2, i * P:(i + 1) * P], qq[:, i, j * P:(j + 1) * P],
                                                    keys[:, 4 * s + i, :], start=True, stop=True)
                        last.then_inc(keys_scored, 1)
                    if w:
                        beside(beside_query(4 * s + 3))

            pe.wait_ge(xT_landed, 16)
            pe.wait_ge(rope_landed, 32)
            project(0, WAVES[0])
            diff_0()
            turn_mixed(0)
            out_half(0, 0)
            out_half(0, 1)
            turn_x1(0)
            query(0, WAVES[0])
            pe.wait_ge(scores_stored, 4)
            pe.wait_ge(xT_rest_landed, 16)
            project(1, WAVES[1])
            diff(1)
            diff(2)
            turn_x1(1)
            pe.wait_ge(x1_taken, 4)
            diff(3)
            turn_x1(2)
            turn_mixed(3)
            beside(beside_mixer(3, 4))
            out_half(3, 0)
            beside(beside_mixer(3, 5))
            out_half(3, 1)
            beside(beside_mixer(3, 6))
            turn_x1(3)
            query(1, WAVES[1])
            for b in range(NB):
                add_block(b)

        @block.scalar
        def _(act):
            fill = [0]

            def take_rotated(w):
                n = rotated[0]
                f = [f for f in FILLS if f[1] in (RQ, RK)][n]
                act.wait_ge(rot_turned, n + 1)
                b = f[2]
                q = b - WAVES[w][0]
                dst = qT[:, :, q * P:(q + 1) * P] if f[1] == RQ else kT[:, :, b * P:(b + 1) * P]
                nc.scalar.activation(dst, W[:, 3, :].rearrange("p (h t) -> p h t", h=H), ACT.Copy).then_inc(rot_taken, 1)
                rotated[0] += 1

            rotated = [0]

            def project(w, blocks):
                n_tok = len(blocks) * P
                toks = slice(blocks[0] * P, (blocks[-1] + 1) * P)
                for f in [f for f in FILLS if f[0] == w]:
                    n = fill[0]
                    g, part = f[1], f[2]
                    bank = W[:, n % 3, :]
                    if g == RG:
                        act.wait_ge(proj_ready, n + 1)
                        act.wait_ge(rot_ready, rots(n))
                        act.wait_ge(proj_taken_dve, takes(n, "dve"))
                        nc.scalar.activation(work[:, HW:2 * HW], bank, ACT.Tanh, scale=0.5).then_inc(tanh_ready, 1)
                    elif g not in (RQ, RK):
                        act.wait_ge(proj_ready, n + 1)
                        if g == RV:
                            dst, src = rv[:, part, :], bank
                        elif g == DV:
                            dst, src = dv[:, part, :], bank
                        elif part is None:
                            src = bank.rearrange("p (h t) -> p h t", h=H)
                            dst = dqT[:, :, 0:P] if g == DQ else dkT[:, :, 0:P]
                        else:
                            src = bank[:, 0:n_tok]
                            dst = dqT[:, part, :] if g == DQ else dkT[:, part, toks]
                        nc.scalar.activation(dst, src, ACT.Copy).then_inc(proj_taken_act, 1)
                    fill[0] += 1
                    if n and FILLS[n - 1][0] == w and FILLS[n - 1][1] in (RQ, RK):
                        take_rotated(w)
                    if w == 0 and g == DKK:
                        act.wait_ge(lam_dots_ready, 1)
                        nc.scalar.activation(lam[:, 2:4], lam[:, 0:2], ACT.Exp).then_inc(lam_exp_ready, 1)
                        act.wait_ge(max_ready, H)
                        for i in range(2 * H):
                            last = nc.scalar.activation(
                                probs[:, i // H, i % H * P:(i % H + 1) * P], X[:, i * P:(i + 1) * P], ACT.Exp,
                                bias=nmax[:, i:i + 1], scale=DK ** -0.5, accum_out=zsum[:, i:i + 1])
                        last.then_inc(exps_ready, H)

            def diagonals(n, odd, weight, slots=PE_SLOTS):
                for r in slots:
                    m = PE_SLOTS.index(r)
                    act.wait_ge(slot_used[r], n)
                    nc.scalar.sem_inc(diag_tick, 1)
                    nc.scalar.activation(diag[:, odd, m, :], ident[:], ACT.Copy,
                                         scale=gate[:, bass.ds(weight(r), 1)]).then_inc(diag_ready, 1)

            def beside(halves):
                for k in halves:
                    n = AT_V + k // 2
                    if n < AT_MIXED:
                        diagonals(n, n % 2, lambda r: (n - AT_V) * RING + r, pe_slots(k))
                    else:
                        diagonals(n, n % 2, lambda r: E - LAG + (n - AT_MIXED) * HALF + r // 2, pe_slots(k))

            def mixed_diagonals(lo, hi):
                def group(i, at):
                    diagonals(i + (AT_MIXED + at), (AT_MIXED + at) % 2, lambda r: i * HALF + (E - LAG + at * HALF + r // 2))
                pairs = (hi - lo) // 2
                if pairs:
                    with act.Fori(0, pairs) as i:
                        for j in range(2):
                            group(i * 2, lo + j)
                if (hi - lo) % 2:
                    group(0, hi - 1)

            def attention(b):
                keys_n = (b + 1) * P
                for h in range(H):
                    n = H * b + h
                    act.wait_ge(max_ready, n + 1)
                    act.wait_ge(a_turned, n)
                    for c in range(2):
                        last = nc.scalar.activation(probs[:, c, 0:keys_n], W[:, c, 0:keys_n], ACT.Exp,
                                                    bias=nmax[:, c:c + 1], scale=DK ** -0.5, accum_out=zsum[:, c:c + 1])
                    last.then_inc(exps_ready, 1)
                    if b > 1 and h == 0:
                        take_mixed(b - 1)
                    beside(beside_mixer(b, h))
                    act.wait_ge(a_turned, n + 1)
                    nc.scalar.activation(aT[:, 0:keys_n], W[:, 3, 0:keys_n], ACT.Copy).then_inc(a_taken, 1)
                squares(b)

            def squares(b):
                act.wait_ge(diff_mixed, b + 1)
                for h in range(H):
                    last = nc.scalar.activation(probs[:, 1, h * P:(h + 1) * P], W[:, 2, h * P:(h + 1) * P], ACT.Square,
                                                accum_out=ssq[:, h:h + 1])
                last.then_inc(squares_ready, 1)

            def take_mixed(b):
                for half in range(2):
                    act.wait_ge(mix_turned, 2 * b + half + 1)
                    nc.scalar.activation(mixT[:, 4 * half:4 * half + 4, :],
                                         out_banks(b, 0)[half].rearrange("p (k t) -> p k t", k=4),
                                         ACT.Copy).then_inc(mix_taken, 1)

            def take_x1(b):
                for half in range(2):
                    act.wait_ge(x1_turned, 2 * b + half + 1)
                    nc.scalar.activation(actT[:, 4 * half:4 * half + 4, b * P:(b + 1) * P],
                                         out_banks(b, 0)[half].rearrange("p (k t) -> p k t", k=4),
                                         ACT.Copy).then_inc(x1_taken, 1)

            def query(w, blocks):
                n_tok = len(blocks) * P
                for n in range(4, 20) if w else range(4):
                    act.wait_ge(query_ready, n + 1)
                    if w and n % 4 == 0 and n > 4:
                        act.wait_ge(keys_scored, 4 + (n // 4 - 1) * 3)
                    if not w and n:
                        act.wait_ge(keys_scored, n)
                    src = W[:, 2 + n % 2, :]
                    if w:
                        dst, src = qq[:, n % 4, 0:n_tok], src[:, 0:n_tok]
                    else:
                        dst, src = qq[:, :, 0:P], src.rearrange("p (i t) -> p i t", i=4)
                    nc.scalar.activation(dst, src, ACT.Copy).then_inc(query_taken, 1)
                    if w:
                        beside(beside_query(n - 4))
                    if not w or n % 4 == 3:
                        s = n // 4 - 1 if w else n
                        for j, b in enumerate(blocks):
                            m = (4 + 3 * s if w else s) + j
                            act.wait_ge(keys_scored, m + 1)
                            nc.scalar.activation(scores[b][:, s * HW:(s + 1) * HW], W[:, m % 2, :],
                                                 ACT.Copy).then_inc(scores_stored, 1)

            def token_to_psum(b):
                act.wait_ge(x1_ready, b + 1)
                if b:
                    last_dot(b * 4 - 1)
                if b == 1:
                    act.wait_ge(x1_taken, 2 * NB)
                for half in range(2):
                    last = nc.scalar.activation(X[:, half * HW:(half + 1) * HW], xs[:, b, half * HW:(half + 1) * HW],
                                                ACT.Copy)
                last.then_inc(token_in_psum, 1)

            def last_dot(q):
                if q < 4:
                    act.wait_ge(slot_used[RING - 1], (q + 1) * QUARTER // RING + 1)
                else:
                    act.wait_ge(slot_used[RING - 2], AT_MIXED + (q - 3) * PERIOD + 1)

            def gelu(lo, hi):
                cols = slice(lo * QUARTER, hi * QUARTER)
                act.wait_ge(experts_ready, hi)
                nc.scalar.activation(gate[:, cols], gate[:, cols], ACT.Exp).then_inc(gate_exp_ready, 1)
                last_dot(hi - 1)
                nc.scalar.activation(hid[:, cols], hid[:, cols], ACT.Gelu).then_inc(gelu_ready, 1)

            project(0, WAVES[0])
            act.wait_ge(a_turned, H)
            nc.scalar.activation(aT, ACC[:, HW:2 * HW], ACT.Copy).then_inc(a_taken, H)
            squares(0)
            take_mixed(0)
            take_x1(0)
            token_to_psum(0)
            query(0, WAVES[0])
            project(1, WAVES[1])
            attention(1)
            attention(2)
            take_x1(1)
            gelu(0, 4)
            act.wait_ge(weights_ready, 1)
            attention(3)
            take_x1(2)
            take_mixed(3)
            for step in range(4, 7):
                beside(beside_mixer(3, step))
            take_x1(3)
            token_to_psum(1)
            query(1, WAVES[1])
            for q in range(4, 4 * NB):
                first = (q - 4) * PERIOD
                if q == 4:
                    mixed_diagonals(PE_BESIDE, PERIOD)
                    continue
                if q % 4 == 0:
                    token_to_psum(q // 4)
                mixed_diagonals(first, first + 1)
                gelu(q - 1, q)
                mixed_diagonals(first + 1, first + 2)
                act.wait_ge(weights_ready, q - 3)
                mixed_diagonals(first + 2, first + PERIOD)
            gelu(4 * NB - 1, 4 * NB)
            for i in range(TAIL):
                if i == 1:
                    act.wait_ge(weights_ready, 4 * NB - 3)
                diagonals(AT_TAIL + i, (AT_TAIL + i) % 2, lambda r: NB * E - LAG + i * RING + r)

        @block.vector
        def _(dve):
            steps = [0]

            def link(ins):
                steps[0] += 1
                ins.then_inc(dve_step, 1)
                dve.wait_ge(dve_step, steps[0])

            def links(made):
                for ins in made:
                    steps[0] += 1
                    ins.then_inc(dve_step, 1)
                dve.wait_ge(dve_step, steps[0])

            TT = nc.vector.tensor_tensor
            TS = nc.vector.tensor_scalar
            STT = nc.vector.scalar_tensor_tensor

            def dot(r, n, e):
                dve.wait_ge(row_landed[r], n * 16 + 16)
                STT(out=ring[:, r, :], in0=ring[:, r, :], scalar=1.0, in1=X[:], op0=ALU.mult, op1=ALU.mult,
                    accum_out=hid[:, bass.ds(e, 1)]).then_inc(slot_used[r], 1)

            def dots(k):
                if k == 0:
                    dve.wait_ge(token_in_psum, 1)
                for r in range(k % 2 * HALF, (k % 2 + 1) * HALF):
                    dot(r, k // 2, k // 2 * RING + r)

            def add_halves(b, r, n, e, added, last_slot, last_count):
                w = gate[:, bass.ds(e, 1)]
                dve.wait_ge(row_landed[r], n * 16 + 16)
                if added:
                    dve.wait_ge(low_added, added)
                STT(out=xs[:, b, 0:HW], in0=ring[:, r, 0:HW], scalar=w, in1=xs[:, b, 0:HW],
                    op0=ALU.mult, op1=ALU.add).then_inc(low_added, 1)
                dve.wait_ge(slot_used[last_slot], last_count)
                STT(out=xs[:, b, HW:D], in0=ring[:, r, HW:D], scalar=w, in1=xs[:, b, HW:D],
                    op0=ALU.mult, op1=ALU.add).then_inc(slot_used[r], 1)

            def sums(lo, hi):
                for k in range(lo, hi):
                    i = k // 2
                    before = dve_slots(i - 1) if i else DVE_SLOTS
                    for m, r in enumerate(dve_slots(i)):
                        if r // HALF == k % 2:
                            n = i + AT_V
                            last = dve_slots(i)[m - 1] if m else before[-1]
                            add_halves(0, r, n, i * RING + r, sum(len(dve_slots(g)) for g in range(i)) + m,
                                       last, n + 2 if m else n + 1)

            def mixed(b, lo, hi):
                with dve.Fori(0, hi - lo) as i:
                    n = i + (AT_MIXED + lo)
                    for r in range(0, DVE_SLOT, 2):
                        dot(r, n, i * HALF + (E + lo * HALF + r // 2))
                    r = DVE_SLOT
                    dve.wait_ge(row_landed[r], n * 16 + 16)
                    dve.wait_ge(slot_used[r], n + 1)
                    e = i * HALF + (E - LAG + lo * HALF + r // 2)
                    STT(out=xs[:, b, :], in0=ring[:, r, :], scalar=gate[:, bass.ds(e, 1)], in1=xs[:, b, :],
                        op0=ALU.mult, op1=ALU.add).then_inc(slot_used[r], 1)
                    for r in range(DVE_SLOT + 1, RING, 2):
                        dot(r, n, i * HALF + (E + lo * HALF + r // 2))

            def tail(lo, hi):
                for i in range(lo, hi):
                    n = AT_TAIL + i
                    for m, r in enumerate(DVE_SLOTS):
                        last = DVE_SLOTS[m - 1] if m or i else DVE_SLOT
                        added = sum(len(dve_slots(g)) for g in range(V_GROUPS)) + i * len(DVE_SLOTS) + m
                        add_halves(NB - 1, r, n, NB * E - LAG + i * RING + r, added, last, n + 2 if m else n + 1)

            def weights(lo, hi):
                cols = slice(lo * QUARTER, hi * QUARTER)
                calls = max(hi - 3, 1)
                dve.wait_ge(gate_exp_ready, calls)
                heads = (hi - lo) * 2
                g = gate[:, cols].rearrange("p (h k) -> p h k", h=heads)
                link(nc.vector.reduce_sum(gsum[:, 0:heads], g, AX.X))
                link(nc.vector.reciprocal(gsum[:, 0:heads], gsum[:, 0:heads]))
                link(TT(out=g, in0=g, in1=gsum[:, 0:heads].unsqueeze(2).to_broadcast([P, heads, TOPK]), op=ALU.mult))
                dve.wait_ge(gelu_ready, calls)
                TT(out=gate[:, cols], in0=gate[:, cols], in1=hid[:, cols], op=ALU.mult).then_inc(weights_ready, 1)
                dve.wait_ge(weights_ready, calls)

            def residual(b):
                link(TS(xs[:, b, :], xs[:, b, :], ALPHA, None, ALU.mult))

            def inverse_root(n):
                v, y, t = rstd[:, 0:n], root[:, 0, 0:n], root[:, 1, 0:n]
                link(TS(t.bitcast(i32), v.bitcast(i32), 1, None, ALU.arith_shift_right))
                link(TS(y.bitcast(i32), t.bitcast(i32), -1.0, float(0x5F3759DF), ALU.mult, ALU.add))
                for step in range(3):
                    link(STT(out=t, in0=y, scalar=-0.5, in1=y, op0=ALU.mult, op1=ALU.mult))
                    link(TT(out=t, in0=t, in1=v, op=ALU.mult))
                    link(STT(out=v if step == 2 else y, in0=t, scalar=1.5, in1=y, op0=ALU.add, op1=ALU.mult))

            def normalise(b, src, gain_bias):
                links([nc.vector.bn_stats(st[:, half, :], src[:, half * HW:(half + 1) * HW]) for half in range(2)])
                link(nc.vector.bn_aggr(mv[:, 0, :], st[:, 0:2, :].rearrange("p a b -> p (a b)")))
                link(TS(rstd[:, 0:1], mv[:, 0, 1:2], EPS, None, ALU.add))
                inverse_root(1)
                link(TS(xs[:, b, :], src, mv[:, 0, 0:1], rstd[:, 0:1], ALU.subtract, ALU.mult))
                link(TT(out=xs[:, b, :], in0=xs[:, b, :], in1=gain_bias[:, 0, :], op=ALU.mult))
                return TT(out=xs[:, b, :], in0=xs[:, b, :], in1=gain_bias[:, 1, :], op=ALU.add)

            def join_sums(b):
                if b < NB - 1:
                    n, slots = AT_MIXED + turn_of(b + 1), (DVE_SLOT, PE_SLOTS[-1])
                else:
                    n, slots = AT_TAIL + TAIL, (DVE_SLOTS[-1], PE_SLOTS[-1])
                for r in slots:
                    dve.wait_ge(slot_used[r], n + 1)
                TT(out=xs[:, b, :], in0=xs[:, b, :], in1=ACC[:], op=ALU.add).then_inc(sum_read, 1)
                dve.wait_ge(sum_read, b + 1)

            def finish(b):
                dve.wait_ge(ln2_landed, 32)
                normalise(b, xs[:, b, :], lng).then_inc(block_done, 1)

            def rotary(n):
                b = FILLS[n][2]
                src = W[:, n % 3, :].rearrange("p (h n) -> p h n", h=H)
                a = work[:, 0:HW].rearrange("p (h n) -> p h n", h=H)
                t = work[:, HW:2 * HW].rearrange("p (h n) -> p h n", h=H)
                cos = rp[:, 0, b, :].unsqueeze(1).to_broadcast([P, H, 64])
                sin = rp[:, 1, b, :].unsqueeze(1).to_broadcast([P, H, 64])
                dve.wait_ge(proj_ready, n + 1)
                if rots(n):
                    dve.wait_ge(rot_turned, rots(n))
                links([TT(out=a[:, :, 0:64], in0=src[:, :, 0:64], in1=cos, op=ALU.mult),
                       TT(out=a[:, :, 64:P], in0=src[:, :, 64:P], in1=cos, op=ALU.mult),
                       TT(out=t[:, :, 0:64], in0=src[:, :, 64:P], in1=sin, op=ALU.mult)])
                TT(out=t[:, :, 64:P], in0=src[:, :, 0:64], in1=sin, op=ALU.mult).then_inc(proj_taken_dve, 1)
                dve.wait_ge(proj_taken_dve, takes(n + 1, "dve"))
                link(TT(out=a[:, :, 0:64], in0=a[:, :, 0:64], in1=t[:, :, 0:64], op=ALU.subtract))
                TT(out=a[:, :, 64:P], in0=a[:, :, 64:P], in1=t[:, :, 64:P], op=ALU.add).then_inc(rot_ready, 1)

            def swish_gate(n):
                w, b = FILLS[n][0], FILLS[n][2]
                dve.wait_ge(tanh_ready, gates(n) + 1)
                STT(out=swish[:, b - WAVES[w][0], :], in0=work[:, HW:2 * HW], scalar=1.0, in1=W[:, n % 3, :],
                    op0=ALU.add, op1=ALU.mult).then_inc(proj_taken_dve, 1)

            def fills_of(w, g):
                return [n for n, f in enumerate(FILLS) if f[0] == w and f[1] == g]

            def decay_scores(b, jb):
                off = b - jb
                dve.wait_ge(ret_scored, tiles_before(b) + jb + 1)
                src = ACC[:, jb % 2 * HW:(jb % 2 + 1) * HW]
                if off < 2:
                    TT(out=sT[:, jb, :], in0=src, in1=dec[:, off, :], op=ALU.mult).then_inc(ret_decayed, 1)
                else:
                    for h in range(H):
                        ins = STT(out=sT[:, jb, h * P:(h + 1) * P], in0=src[:, h * P:(h + 1) * P],
                                  scalar=decay_far[h] ** (off - 1), in1=dec[:, 1, h * P:(h + 1) * P],
                                  op0=ALU.mult, op1=ALU.mult)
                    ins.then_inc(ret_decayed, 1)

            def retention_norm(b):
                R = W[:, 3, :]
                q = b - (b > 0)
                dve.wait_ge(ret_mixed, b + 1)
                links([nc.vector.bn_stats(st[:, h, :], R[:, h * P:(h + 1) * P]) for h in range(H)])
                links([nc.vector.bn_aggr(mv[:, h, :], st[:, h, :]) for h in range(H)])
                link(TS(rstd[:], mv[:, :, 1], EPS, None, ALU.add))
                inverse_root(H)
                for h in range(H):
                    ins = TS(work[:, h * P:(h + 1) * P], R[:, h * P:(h + 1) * P], mv[:, h, 0:1], rstd[:, h:h + 1],
                             ALU.subtract, ALU.mult)
                    if h == H - 1:
                        ins.then_inc(ret_normed, 1)
                dve.wait_ge(ret_normed, b + 1)
                link(TT(out=work[:, 0:HW], in0=work[:, 0:HW], in1=gn[:, 0, :], op=ALU.mult))
                link(TT(out=work[:, 0:HW], in0=work[:, 0:HW], in1=gn[:, 1, :], op=ALU.add))
                link(TT(out=swish[:, q, :], in0=work[:, 0:HW], in1=swish[:, q, :], op=ALU.mult))

            def softmax_max(b, h):
                keys_n = (b + 1) * P
                dve.wait_ge(diff_scored, H * b + h + 1)
                link(TT(out=W[:, 0:2, b * P:keys_n], in0=W[:, 0:2, b * P:keys_n],
                        in1=mask[:].unsqueeze(1).to_broadcast([P, 2, P]), op=ALU.add))
                link(nc.vector.reduce_max(smax[:, 0:2], W[:, 0:2, 0:keys_n], AX.X))
                TS(nmax[:, 0:2], smax[:, 0:2], -DK ** -0.5, None, ALU.mult).then_inc(max_ready, 1)

            def softmax_join(b, h):
                keys_n = (b + 1) * P
                dve.wait_ge(exps_ready, H * b + h + 1)
                link(nc.vector.reciprocal(rz[:, 0:2], zsum[:, 0:2]))
                link(TS(rz[:, 1:2], rz[:, 1:2], lam[:, 0:1], None, ALU.mult))
                link(TS(probs[:, 1, 0:keys_n], probs[:, 1, 0:keys_n], rz[:, 1:2], None, ALU.mult))
                STT(out=probs[:, 0, 0:keys_n], in0=probs[:, 0, 0:keys_n], scalar=rz[:, 0:1], in1=probs[:, 1, 0:keys_n],
                    op0=ALU.mult, op1=ALU.add).then_inc(a_ready, 1)

            def softmax_max_0():
                dve.wait_ge(diff_scored, H)
                tiles = X[:].rearrange("p (i t) -> p i t", i=2 * H)
                link(TT(out=tiles, in0=tiles, in1=mask[:].unsqueeze(1).to_broadcast([P, 2 * H, P]), op=ALU.add))
                link(nc.vector.reduce_max(smax[:], tiles, AX.X))
                TS(nmax[:], smax[:], -DK ** -0.5, None, ALU.mult).then_inc(max_ready, H)

            def softmax_join_0():
                dve.wait_ge(exps_ready, H)
                link(nc.vector.reciprocal(rz[:], zsum[:]))
                link(TS(rz[:, H:2 * H], rz[:, H:2 * H], lam[:, 0:1], None, ALU.mult))
                both = probs.rearrange("p c (h t) -> p c h t", h=H)
                scale = rz[:].rearrange("p (c h) -> p c h", c=2)
                links([TT(out=both[:, c], in0=both[:, c], in1=scale[:, c, :].unsqueeze(2).to_broadcast([P, H, P]),
                          op=ALU.mult) for c in range(2)])
                TT(out=probs[:, 0, :], in0=probs[:, 0, :], in1=probs[:, 1, :], op=ALU.add).then_inc(a_ready, H)

            def diff_norm(b):
                dve.wait_ge(squares_ready, b + 1)
                if b:
                    dve.wait_ge(mix_turned, 2 * b)
                link(TS(rstd[:], ssq[:], 1.0 / P, EPS, ALU.mult, ALU.add))
                inverse_root(H)
                for h in range(H):
                    ins = STT(out=work[:, HW + h * P:HW + (h + 1) * P], in0=W[:, 2, h * P:(h + 1) * P],
                              scalar=rstd[:, h:h + 1], in1=gn[:, 2, h * P:(h + 1) * P], op0=ALU.mult, op1=ALU.mult)
                ins.then_inc(mix_ready, 1)

            def ln1(b):
                if b == 1:
                    dve.wait_ge(x_rest_landed, 16)
                dve.wait_ge(mixer_ready, 2 * (b + 1))
                src = W[:, 2:4, :].rearrange("p a n -> p (a n)") if b == 0 else ACC[:] if b == 1 else X[:]
                link(STT(out=xs[:, b, :], in0=xs[:, b, :], scalar=ALPHA, in1=src, op0=ALU.mult, op1=ALU.add))
                normalise(b, xs[:, b, :], lng).then_inc(x1_ready, 1)

            def retrieve(b, s):
                best_keys(b, s)
                best_pairs()
                best_experts(b, s)

            def best_keys(b, s):
                dve.wait_ge(scores_stored, 4 + 3 * s + b if b else s + 1)
                sc = [scores[b][:, s * HW + i * P:s * HW + (i + 1) * P] for i in range(4)]
                left = [cand[:, i * P:(i + 1) * P] for i in range(4)]
                links([nc.vector.max(best_v[:, i, 0:8], sc[i]) for i in range(4)])
                links([nc.vector.match_replace(left[i], best_v[:, i, 0:8], sc[i], LOWEST) for i in range(4)])
                links([nc.vector.max_index(best_i[:, i, 0:8], best_v[:, i, 0:8], sc[i]) for i in range(4)]
                      + [nc.vector.max(best_v[:, i, 8:16], left[i]) for i in range(4)])
                links([nc.vector.max_index(best_i[:, i, 8:16], best_v[:, i, 8:16], left[i]) for i in range(4)])

            def best_pairs():
                v = best_v[:].rearrange("p (h c) k -> p h c k", c=2)
                link(TT(out=cand[:].rearrange("p (h a b) -> p h a b", h=2, a=TOPK),
                        in0=v[:, :, 0, :].unsqueeze(3).to_broadcast([P, 2, TOPK, TOPK]),
                        in1=v[:, :, 1, :].unsqueeze(2).to_broadcast([P, 2, TOPK, TOPK]), op=ALU.add))
                c = [cand[:, h * 256:(h + 1) * 256] for h in range(2)]
                tp = [top_p[:, h * TOPK:(h + 1) * TOPK] for h in range(2)]
                links([nc.vector.max(top_v[:, h, 0:8], c[h]) for h in range(2)])
                links([nc.vector.max_index(tp[h][:, 0:8], top_v[:, h, 0:8], c[h]) for h in range(2)])
                links([nc.vector.match_replace(c[h], top_v[:, h, 0:8], c[h], LOWEST) for h in range(2)])
                links([nc.vector.max(top_v[:, h, 8:16], c[h]) for h in range(2)])
                links([nc.vector.max_index(tp[h][:, 8:16], top_v[:, h, 8:16], c[h]) for h in range(2)])

            def best_experts(b, s):
                at = b * E + s * QUARTER
                link(nc.vector.tensor_copy(half_f[:], best_i[:]))
                i_f = half_f[:].rearrange("p (h c) k -> p h c k", c=2)
                onehot = cand[:].rearrange("p (e a) -> p e a", a=TOPK)
                pick = cand[:].rearrange("p (h k a) -> p h k a", h=2, k=TOPK)
                n = 2 * TOPK
                halves = ((ALU.logical_shift_right, 4), (ALU.bitwise_and, 15))
                links([TS(pos_u[:, c, :], top_p[:], arg, None, op) for c, (op, arg) in enumerate(halves)])
                link(nc.vector.tensor_copy(pos_f[:], pos_u[:]))
                for c in range(2):
                    link(TT(out=onehot, in0=pos_f[:, c, :].unsqueeze(2).to_broadcast([P, n, TOPK]),
                            in1=iota_f[:].unsqueeze(1).to_broadcast([P, n, TOPK]), op=ALU.is_equal))
                    link(TT(out=pick, in0=pick, in1=i_f[:, :, c, :].unsqueeze(2).to_broadcast([P, 2, TOPK, TOPK]),
                            op=ALU.mult))
                    link(nc.vector.reduce_sum(sel[:, c, :], onehot, AX.X))
                link(TT(out=gate[:, at:at + n].rearrange("p (h k) -> p h k", h=2), in0=top_v[:],
                        in1=top_v[:, :, 0:1].to_broadcast([P, 2, TOPK]), op=ALU.subtract))
                STT(out=idx[:, at:at + n], in0=sel[:, 0, :], scalar=float(P), in1=sel[:, 1, :],
                    op0=ALU.mult, op1=ALU.add).then_inc(experts_ready, 1)

            dve.wait_ge(iota_ready, 1)
            link(nc.vector.tensor_copy(iota_f[:], iota_i[:]))
            dve.wait_ge(rope_landed, 32)

            rotary(fills_of(0, RQ)[0])
            rotary(fills_of(0, RK)[0])
            swish_gate(fills_of(0, RG)[0])
            dve.wait_ge(lam_landed, 64)
            lam_v = lam_in[:].rearrange("p (a b) n -> p a b n", b=2)
            link(TT(out=lam_v[:, :, 0, :], in0=lam_v[:, :, 0, :], in1=lam_v[:, :, 1, :], op=ALU.mult))
            nc.vector.reduce_sum(lam[:, 0:2], lam_v[:, :, 0, :], AX.X).then_inc(lam_dots_ready, 1)
            dve.wait_ge(tabs_landed, 5 * 16)
            link(TS(gn[:, 0:2, :], gn[:, 0:2, :], 0.5, None, ALU.mult))
            link(TS(gn[:, 2, :], gn[:, 2, :], 1.0 - LAMBDA_INIT, None, ALU.mult))
            decay_scores(0, 0)
            retention_norm(0)
            dve.wait_ge(lam_exp_ready, 1)
            link(TT(out=lam[:, 1:2], in0=lam[:, 3:4], in1=lam[:, 2:3], op=ALU.subtract))
            link(TS(lam[:, 0:1], lam[:, 1:2], -LAMBDA_INIT, None, ALU.add))
            softmax_max_0()
            softmax_join_0()
            diff_norm(0)
            dve.wait_ge(x_landed, 16)
            dve.wait_ge(ln1_landed, 32)
            ln1(0)
            taken = [0]

            def rows(n):
                for k in range(taken[0], taken[0] + n):
                    if k < 2 * U_GROUPS:
                        dots(k)
                    else:
                        sums(k - 2 * U_GROUPS, k + 1 - 2 * U_GROUPS)
                taken[0] += n

            retrieve(0, 0)
            retrieve(0, 1)
            for i, n in enumerate(fills_of(1, RQ) + fills_of(1, RK) + fills_of(1, RG)):
                if FILLS[n][1] == RG:
                    rows(2)
                    swish_gate(n)
                else:
                    rows(1)
                    rotary(n)
                if i in (5, 6):
                    retrieve(0, i - 3)
            dve.wait_ge(rot_turned, rots(len(FILLS)))
            rows(1)
            for b in range(1, NB):
                for jb in range(b + 1):
                    decay_scores(b, jb)
                    if jb % 2:
                        rows(1)
                if b > 1:
                    rows(1)
                retention_norm(b)
            for b in range(1, NB):
                for h in range(H):
                    softmax_max(b, h)
                    if b == NB - 1:
                        rows(BESIDE_MIXER[h])
                    elif taken[0] < 2 * U_GROUPS:
                        rows(1)
                    softmax_join(b, h)
                if b > 1:
                    ln1(b - 1)
                diff_norm(b)
                if b == 2:
                    rows(2 * U_GROUPS - taken[0])
                    weights(0, 4)
                    residual(0)
            rows(sum(BESIDE_MIXER[H:]) - 1)
            ln1(3)
            scored = 17
            sums(taken[0] - 2 * U_GROUPS, scored)
            retrieve(1, 0)
            sums(scored, 2 * V_GROUPS)
            dve.wait_ge(slot_used[dve_slots(V_GROUPS - 1)[-1]], AT_MIXED + 1)

            for q in range(4, 4 * NB):
                b, s = divmod(q + 1, 4)
                first = (q - 4) * PERIOD
                if q % 4 == 0:
                    dve.wait_ge(token_in_psum, q // 4 + 1)
                summed = (E - LAG + first * HALF) // E
                mixed(summed, first, first + 1)
                if q > 4:
                    weights(q - 1, q)
                mixed(summed, first + 1, first + 2)
                turn = first + 2 == turn_of(summed + 1)
                if turn:
                    join_sums(summed)
                    summed += 1
                    residual(summed)
                for i, step in enumerate((lambda: best_keys(b, s), best_pairs, lambda: best_experts(b, s))):
                    if b < NB:
                        step()
                    mixed(summed, first + 2 * i + 2, first + 2 * i + 4)
                    if i == 1 and turn:
                        finish(summed - 1)
            dve.wait_ge(slot_used[DVE_SLOT], AT_TAIL + 1)
            tail(0, 1)
            weights(4 * NB - 1, 4 * NB)
            tail(1, TAIL)
            join_sums(NB - 1)
            finish(NB - 1)


def constants():
    import numpy as np
    log_g = np.log1p(-(2.0 ** (-5.0 - np.arange(H))))
    i = np.arange(P)
    rel = (i[None, :] - i[:, None])[:, None, :]
    near = np.where(rel >= 0, np.exp(np.maximum(rel, 0) * log_g[None, :, None]), 0.0)
    far = np.exp((rel + P) * log_g[None, :, None])
    decay = (np.stack([near, far], axis=1) * P ** -0.5).reshape(P, 2, HW)
    ang = np.arange(S)[:, None] * (10000.0 ** (-np.arange(64) / 64.0))[None, :]
    rope = np.stack([np.cos(ang), np.sin(ang)])
    mask = np.where(i[None, :] > i[:, None], MASKED, 0.0)
    f = np.float32
    return {"decay": decay.astype(f), "rope": rope.astype(f), "ident_in": np.eye(P, dtype=f),
            "mask_in": mask.astype(f)}, [float(v) for v in np.exp(P * log_g)]


INPUTS = ["x", "xT", "w_in", "ret_gn_g", "ret_gn_b", "diff_lambda_q1", "diff_lambda_k1", "diff_lambda_q2",
          "diff_lambda_k2", "diff_subln_g", "w_out", "ln1_g", "ln1_b", "peer_w_query", "keysT", "peer_u",
          "peer_v", "ln2_g", "ln2_b", "decay", "rope", "ident_in", "mask_in"]


def kernel(**inputs):
    import numpy as np
    import concourse.bacc as bacc
    from concourse.bass_utils import run_bass_kernel_spmd

    given = {n: np.asarray(a)[0] for n, a in inputs.items()}
    given["xT"] = given["x"].T
    given["keysT"] = given["peer_sub_keys"].transpose(3, 0, 1, 2).reshape(P, HC, P)
    tables, decay_far = constants()
    given.update(tables)
    nc = bacc.Bacc("TRN2", target_bir_lowering=False, num_devices=1)
    arrays, aps = {}, []
    for name in INPUTS:
        a = np.ascontiguousarray(given[name])
        arrays[name] = a
        aps.append(nc.dram_tensor(name, a.shape, mybir.dt.from_np(a.dtype), kind="ExternalInput").ap())
    out = nc.dram_tensor("out", (S, D), fp32, kind="ExternalOutput").ap()
    build(nc, *aps, decay_far, out)
    r = run_bass_kernel_spmd(nc, [arrays], core_ids=[0])
    return r.results[0]["out"].reshape(1, S, D)
```
